# Optimizing a Trainium2 kernel written in Bass

```python
import jax, jax.numpy as jnp
from jax import lax
import numpy as np

D_MODEL = 1024
BATCH = 1
SEQ = 128
DEPTH = 2
DEC_BATCH = 1
DEC_SEQ = 1024
PAST_LEN = 128

GRID_W = 64
MLA_HEADS = 6
MLA_Q_RANK = 384
MLA_KV_RANK = 256
MLA_NOPE_DIM = 64
MLA_ROPE_DIM = 32
MLA_V_DIM = 64
MLA_QK_DIM = MLA_NOPE_DIM + MLA_ROPE_DIM
MLA_WIDTH = MLA_HEADS * MLA_V_DIM
FNET_GROUPS = 4
FNET_GROUP_DIM = 64
FNET_WIDTH = FNET_GROUPS * FNET_GROUP_DIM
GQA_HEADS = 6
GQA_KV_HEADS = 2
GQA_HEAD_DIM = 64
GQA_GROUP = GQA_HEADS // GQA_KV_HEADS
GQA_WIDTH = GQA_HEADS * GQA_HEAD_DIM
MIX_WIDTH = MLA_WIDTH + FNET_WIDTH + GQA_WIDTH
IN_SIZES = (MLA_Q_RANK, MLA_KV_RANK, MLA_ROPE_DIM, FNET_WIDTH,
            GQA_WIDTH, GQA_KV_HEADS * GQA_HEAD_DIM, GQA_KV_HEADS * GQA_HEAD_DIM)
IN_WIDTH = sum(IN_SIZES)
D_FF = -(-8 * D_MODEL // (3 * 256)) * 256
ROPE_THETA = 10000.0
EPS = 1e-6
Q_BLOCK = 128

kernel_name = "hybrid_mla_fnet_gqa_diffusion_step"

def rms_norm(x, g):
    xf = x.astype(jnp.float32)
    y = xf * lax.rsqrt(jnp.mean(xf * xf, axis=-1, keepdims=True) + EPS)
    return (y * g.astype(jnp.float32)).astype(x.dtype)

def grid_angles(n_tokens, rot_dim):
    rows = n_tokens // GRID_W
    row = jnp.repeat(jnp.arange(rows, dtype=jnp.float32), GRID_W)
    col = jnp.tile(jnp.arange(GRID_W, dtype=jnp.float32), rows)
    n_axis = rot_dim // 4
    inv = ROPE_THETA ** (-jnp.arange(n_axis, dtype=jnp.float32) / n_axis)
    return jnp.concatenate([row[:, None] * inv, col[:, None] * inv], axis=-1)

def apply_rope(x, ang):
    half = x.shape[-1] // 2
    cos = jnp.cos(ang)[None, :, None, :]
    sin = jnp.sin(ang)[None, :, None, :]
    x1 = x[..., :half].astype(jnp.float32)
    x2 = x[..., half:].astype(jnp.float32)
    return jnp.concatenate([x1 * cos - x2 * sin, x2 * cos + x1 * sin], axis=-1).astype(x.dtype)

def block_attention(q, k, v, scale):
    b, sq = q.shape[:2]
    nb = sq // Q_BLOCK
    qb = q.reshape((b, nb, Q_BLOCK) + q.shape[2:]).swapaxes(0, 1)

    def one_block(qi):
        s = jnp.einsum('bqhgd,bkhd->bhgqk', qi, k, preferred_element_type=jnp.float32) * scale
        p = jax.nn.softmax(s, axis=-1)
        return jnp.einsum('bhgqk,bkhe->bqhge', p.astype(v.dtype), v)

    out = lax.map(one_block, qb)
    return out.swapaxes(0, 1).reshape((b, sq) + out.shape[3:])

def token_mixers(h, w_in, g_q_a, w_q_up, g_kv_a, w_kv_up, g_q_head, g_k_head, w_out, ctx):
    b, s, _ = h.shape
    proj = h @ w_in
    offs = [int(o) for o in np.cumsum(IN_SIZES)[:-1]]
    cq, ckv, krope, u, gq, gk, gv = jnp.split(proj, offs, axis=-1)

    q_mla = (rms_norm(cq, g_q_a) @ w_q_up).reshape(b, s, MLA_HEADS, MLA_QK_DIM)
    q_nope, q_rope = q_mla[..., :MLA_NOPE_DIM], q_mla[..., MLA_NOPE_DIM:]
    ckv = rms_norm(ckv, g_kv_a)
    krope = krope[:, :, None, :]
    gq = rms_norm(gq.reshape(b, s, GQA_HEADS, GQA_HEAD_DIM), g_q_head)
    gk = rms_norm(gk.reshape(b, s, GQA_KV_HEADS, GQA_HEAD_DIM), g_k_head)
    gv = gv.reshape(b, s, GQA_KV_HEADS, GQA_HEAD_DIM)

    if ctx is None:
        new_ctx = (ckv, krope[:, :, 0, :], gk, gv)
        ckv_all, krope_all, gk_all, gv_all = ckv, krope, gk, gv
    else:
        new_ctx = None
        ang_mla = grid_angles(s, MLA_ROPE_DIM)
        ang_gqa = grid_angles(s, GQA_HEAD_DIM)
        q_rope = apply_rope(q_rope, ang_mla)
        krope_l = apply_rope(krope, ang_mla)
        gq = apply_rope(gq, ang_gqa)
        gk_l = apply_rope(gk, ang_gqa)
        c_ckv, c_krope, c_gk, c_gv = ctx
        ckv_all = jnp.concatenate([c_ckv.astype(ckv.dtype), ckv], axis=1)
        krope_all = jnp.concatenate([c_krope[:, :, None, :].astype(krope.dtype), krope_l], axis=1)
        gk_all = jnp.concatenate([c_gk.astype(gk.dtype), gk_l], axis=1)
        gv_all = jnp.concatenate([c_gv.astype(gv.dtype), gv], axis=1)

    sk = ckv_all.shape[1]
    kv = (ckv_all @ w_kv_up).reshape(b, sk, MLA_HEADS, MLA_NOPE_DIM + MLA_V_DIM)
    k_nope, v_mla = kv[..., :MLA_NOPE_DIM], kv[..., MLA_NOPE_DIM:]
    k_mla = jnp.concatenate(
        [k_nope, jnp.broadcast_to(krope_all, (b, sk, MLA_HEADS, MLA_ROPE_DIM))], axis=-1)
    q_full = jnp.concatenate([q_nope, q_rope], axis=-1)[:, :, :, None, :]
    mla_out = block_attention(q_full, k_mla, v_mla, MLA_QK_DIM ** -0.5).reshape(b, s, MLA_WIDTH)

    uf = u.reshape(b, s, FNET_GROUPS, FNET_GROUP_DIM).astype(jnp.float32)
    fnet_out = jnp.fft.fft2(uf, axes=(1, 3), norm='ortho').real.astype(h.dtype).reshape(b, s, FNET_WIDTH)

    gq5 = gq.reshape(b, s, GQA_KV_HEADS, GQA_GROUP, GQA_HEAD_DIM)
    gqa_out = block_attention(gq5, gk_all, gv_all, GQA_HEAD_DIM ** -0.5).reshape(b, s, GQA_WIDTH)

    out = jnp.concatenate([mla_out, fnet_out, gqa_out], axis=-1) @ w_out
    return out, new_ctx

def trunk_layer(x, mod, g1, g2, w_in, g_q_a, w_q_up, g_kv_a, w_kv_up, g_q_head, g_k_head,
                w_out, w_gate, w_up, w_down, ctx):
    shift1, scale1, gate1, shift2, scale2, gate2 = jnp.split(mod.astype(x.dtype), 6, axis=-1)
    h = rms_norm(x, g1) * (1 + scale1) + shift1
    mix, new_ctx = token_mixers(h, w_in, g_q_a, w_q_up, g_kv_a, w_kv_up, g_q_head, g_k_head,
                                w_out, ctx)
    x = x + gate1 * mix
    h = rms_norm(x, g2) * (1 + scale2) + shift2
    x = x + gate2 * ((jax.nn.silu(h @ w_gate) * (h @ w_up)) @ w_down)
    return x, new_ctx

def setup_inputs(seed: int = 0) -> dict:
    key = jax.random.key(seed)
    ks = jax.random.split(key, 26)

    def nrm(k, shape, scale):
        return jax.random.normal(k, shape, jnp.float32) * scale

    def gain(k, shape):
        return 1.0 + 0.05 * jax.random.normal(k, shape, jnp.float32)

    return {
        "x_prompt": nrm(ks[0], (BATCH, SEQ, D_MODEL), 1.0),
        "x_sample": nrm(ks[1], (DEC_BATCH, DEC_SEQ, D_MODEL), 1.0),
        "cache_mla_ckv": nrm(ks[2], (DEC_BATCH, DEPTH, PAST_LEN, MLA_KV_RANK), 1.0),
        "cache_mla_krope": nrm(ks[3], (DEC_BATCH, DEPTH, PAST_LEN, MLA_ROPE_DIM), 1.0),
        "cache_gqa_k": nrm(ks[4], (DEC_BATCH, DEPTH, PAST_LEN, GQA_KV_HEADS, GQA_HEAD_DIM), 1.0),
        "cache_gqa_v": nrm(ks[5], (DEC_BATCH, DEPTH, PAST_LEN, GQA_KV_HEADS, GQA_HEAD_DIM), 1.0),
        "c": nrm(ks[6], (DEC_BATCH, D_MODEL), 1.0),
        "c_ctx": nrm(ks[7], (D_MODEL,), 1.0),
        "w_ada": nrm(ks[8], (DEPTH, D_MODEL, 6 * D_MODEL), 0.5 * D_MODEL ** -0.5),
        "b_ada": nrm(ks[9], (DEPTH, 6 * D_MODEL), 0.01),
        "g_norm1": gain(ks[10], (DEPTH, D_MODEL)),
        "g_norm2": gain(ks[11], (DEPTH, D_MODEL)),
        "w_in": nrm(ks[12], (DEPTH, D_MODEL, IN_WIDTH), D_MODEL ** -0.5),
        "g_q_a": gain(ks[13], (DEPTH, MLA_Q_RANK)),
        "w_q_up": nrm(ks[14], (DEPTH, MLA_Q_RANK, MLA_HEADS * MLA_QK_DIM), MLA_Q_RANK ** -0.5),
        "g_kv_a": gain(ks[15], (DEPTH, MLA_KV_RANK)),
        "w_kv_up": nrm(ks[16], (DEPTH, MLA_KV_RANK, MLA_HEADS * (MLA_NOPE_DIM + MLA_V_DIM)),
                       MLA_KV_RANK ** -0.5),
        "g_q_head": gain(ks[17], (DEPTH, GQA_HEAD_DIM)),
        "g_k_head": gain(ks[18], (DEPTH, GQA_HEAD_DIM)),
        "w_out": nrm(ks[19], (DEPTH, MIX_WIDTH, D_MODEL), MIX_WIDTH ** -0.5),
        "w_ffn_gate": nrm(ks[20], (DEPTH, D_MODEL, D_FF), D_MODEL ** -0.5),
        "w_ffn_up": nrm(ks[21], (DEPTH, D_MODEL, D_FF), D_MODEL ** -0.5),
        "w_ffn_down": nrm(ks[22], (DEPTH, D_FF, D_MODEL), D_FF ** -0.5),
        "g_final": gain(ks[23], (D_MODEL,)),
    }

def reference(x_prompt, x_sample, cache_mla_ckv, cache_mla_krope, cache_gqa_k, cache_gqa_v,
              c, c_ctx, w_ada, b_ada, g_norm1, g_norm2, w_in, g_q_a, w_q_up, g_kv_a, w_kv_up,
              g_q_head, g_k_head, w_out, w_ffn_gate, w_ffn_up, w_ffn_down, g_final):
    xp, xs = x_prompt, x_sample
    silu_ctx = jax.nn.silu(c_ctx)
    silu_c = jax.nn.silu(c)
    ckv_list, krope_list, gk_list, gv_list = [], [], [], []
    for l in range(DEPTH):
        w_l = (g_norm1[l], g_norm2[l], w_in[l], g_q_a[l], w_q_up[l], g_kv_a[l], w_kv_up[l],
               g_q_head[l], g_k_head[l], w_out[l], w_ffn_gate[l], w_ffn_up[l], w_ffn_down[l])
        mod_ctx = (silu_ctx @ w_ada[l] + b_ada[l])[None, None, :]
        xp, (ckv, krope, gk, gv) = trunk_layer(xp, mod_ctx, *w_l, None)
        ckv_list.append(ckv)
        krope_list.append(krope)
        gk_list.append(gk)
        gv_list.append(gv)
        mod_lat = (silu_c @ w_ada[l] + b_ada[l])[:, None, :]
        ctx_l = (cache_mla_ckv[:, l], cache_mla_krope[:, l], cache_gqa_k[:, l], cache_gqa_v[:, l])
        xs, _ = trunk_layer(xs, mod_lat, *w_l, ctx_l)
    y_prompt = rms_norm(xp, g_final)
    y_sample = rms_norm(xs, g_final)
    new_mla_ckv = jnp.stack(ckv_list, axis=1)
    new_mla_krope = jnp.stack(krope_list, axis=1)
    new_gqa_k = jnp.stack(gk_list, axis=1)
    new_gqa_v = jnp.stack(gv_list, axis=1)
    return (y_prompt, y_sample, new_mla_ckv, new_mla_krope, new_gqa_k, new_gqa_v)


_drawn_inputs = setup_inputs


def setup_inputs(seed=0):
    import zlib

    import numpy as np

    out = dict(_drawn_inputs(seed))
    spreads = {}
    factors = {'cache_mla_ckv': 8.0,
     'cache_mla_krope': 8.0,
     'cache_gqa_k': 8.0,
     'cache_gqa_v': 8.0,
     'b_ada': 3.621,
     'g_norm2': 2.911,
     'g_q_a': 8.0,
     'g_q_head': 8.0}
    for name, (base, spread) in spreads.items():
        noise = np.random.default_rng([zlib.crc32(name.encode()), seed]).standard_normal(out[name].shape)
        drawn = base * np.exp(spread * noise) if base else spread * noise
        out[name] = __import__('jax').numpy.asarray(drawn.astype(out[name].dtype))
    for name, factor in factors.items():
        out[name] = (out[name] * factor).astype(out[name].dtype)
    return out
```

```python
from contextlib import ExitStack

import numpy as np

import concourse.bass as bass
from concourse import mybir

F32 = mybir.dt.float32
F32R = mybir.dt.float32r
ALU = mybir.AluOpType
ACT = mybir.ActivationFunctionType
AX_X = mybir.AxisListType.X

P = 128
D_MODEL, DEPTH, EPS = 1024, 2, 1e-6
CTX, LAT, PAST = 128, 1024, 128
T = CTX + LAT
KEYS = CTX + PAST + LAT
KT = KEYS // P
DK = D_MODEL // P
G, GW = 3, T // 3
NOPE, ROPE, VD, HEADS = 64, 32, 64, 6
QR, KVR = 384, 256
D_FF = 2816
CHUNKS = D_FF // (2 * P)
MLA_SCALE = (NOPE + ROPE) ** -0.5
GQA_SCALE = VD ** -0.5
GRID_W = 64

PRE_LOADS = 22
DVE_STEPS = 49
IN_TILES = [("u", 672, 128), ("u", 800, 128), ("cq", 0, 128), ("cq", 128, 128), ("cq", 256, 128),
            ("ckv", 384, 128), ("ckv", 512, 128), ("kr", 640, 32), ("gk", 1312, 128), ("gv", 1440, 128),
            ("gq", 928, 128), ("gq", 1056, 128), ("gq", 1184, 128)]
N_IN, N_DFT, N_QUP, N_KVUP, N_OUT, N_FFN = len(IN_TILES), 2 * (LAT // P), 3, 2, DK, 6 * CHUNKS
U_DFT = N_IN
U_QUP = U_DFT + N_DFT
U_KVUP = U_QUP + N_QUP
U_OUT = U_KVUP + N_KVUP
U_FFN = U_OUT + N_OUT
UNITS = U_FFN + N_FFN
RING, STAGES = 6, 3


def loads_through(u):
    return sum(2 if U_QUP <= v < U_OUT else 1 for v in range(u % STAGES, u + 1, STAGES))


STAGE_LOADS = [loads_through(UNITS - STAGES + s) for s in range(STAGES)]
assert UNITS % RING == 0 and U_FFN % RING == 0 and RING % STAGES == 0

ROW = {"u": 0, "cq": 256, "ckv": 640, "gk": 896, "gq": 1024}
SCR_ROWS = 1408

E_IN = 0
E_DFT = E_IN + G * N_IN
E_QUP = E_DFT + 9
E_V = E_QUP + 5 * G
E_K = E_V + KT
KGW, KG = KEYS // 4, 4
EVJ = E_K + 3 * KG
EV_SLOTS = 6

R_JOBS = ([("cq", 0, g) for g in range(G)] + [("gk", 0, g) for g in range(G)]
          + [("gq", m, g) for m in range(3) for g in range(G)] + [("ckv", 0, g) for g in range(G)]
          + [("rope", t, g) for t in range(2) for g in range(G)])
R_DFT = 15
R_NORMED = 18
STATS = 2 * G + R_NORMED
RO_SLOTS = 3
R_USES = []
for _r, (_kind, _t, _g) in enumerate(R_JOBS):
    for _i in range({"cq": 3, "ckv": 2}.get(_kind, 1)):
        _n = {"cq": 1, "gq": 1, "gk": 2 if _g == 0 else 1, "ckv": 1 if _g == 0 else 0}.get(_kind)
        if _kind == "rope":
            _n = 1 if _t == 0 else (3 if _g == 0 else 2)
        R_USES.append((_r, _i, _n))
assert len(R_USES) % RO_SLOTS == 0


def ev_stores(e):
    name = IN_TILES[e // G][0] if e < E_DFT else ""
    return 3 if name == "gv" and e % G == 0 else 1


def store_counts(stores, slots):
    total, after = [0] * slots, []
    for n, k in enumerate(stores):
        total[n % slots] += 16 * k
        after.append(total[n % slots])
    return after, total


EV_AFTER, EV_TOTAL = store_counts([ev_stores(e) for e in range(EVJ)], EV_SLOTS)
RO_AFTER, RO_TOTAL = store_counts([k for _, _, k in R_USES], RO_SLOTS)


def r_loads(kind, t):
    return {"cq": 1, "ckv": 1, "gk": 6, "gq": 6}.get(kind) or (10 if t == 0 else 8)


RL_AFTER, RL_TOTAL = store_counts([r_loads(k, t) for k, t, _ in R_JOBS], 2)

TILES, GROUPS = 18, 10
LAST_OF_GROUP = [9 * h + e for h in range(2) for e in (1, 3, 5, 7, 8)]
PAIRS = HEADS
T_CHUNKS = [(0, 3), (3, 4), (7, 2)]


V_ORDER = [0] + list(range(2, KT)) + [1]


def is_ctx(s):
    return s % 9 == 8


def chunk_no(s, c=0):
    return 25 * (s // 9) + 3 * (s % 9) + c


def chunks_of(s):
    return [(0, 0, 1)] if is_ctx(s) else [(c, k0, n) for c, (k0, n) in enumerate(T_CHUNKS)]


def chunks_through(s):
    return chunk_no(s) + len(chunks_of(s))


PAIR_CHUNKS = 50


def group_of(s):
    return 5 * (s // 9) + (s % 9) // 2


def build(nc, a, o):
    ctx = ExitStack()
    with ctx:
        FIRST_BYTE = -(-nc.sbuf_base // 64) * 64
        total = nc.sbuf_bytes_remaining // 64 * 64
        arena = ctx.enter_context(nc.sbuf_tensor("arena", [P, (total - 64) // 4], F32))
        base = FIRST_BYTE
        room = total - 128
        at = [0]

        def place(name, shape, dt, offset):
            return nc.alloc_sbuf_tensor_at(name, shape, dt, offset=base + offset)

        def keep(name, shape, dt=F32):
            size = int(np.prod(shape[1:])) * 4
            size += -size % 32
            at[0] += size
            return place(name, shape, dt, at[0] - size)

        x = keep("x", [P, DK, T])
        w_hi = keep("w_hi", [P, RING, 1024], F32R)
        w_lo = keep("w_lo", [P, RING, 1024], F32R)
        w_in_st = keep("w_stage", [P, STAGES, 1024])
        wk = keep("wk", [P, 4, GW])
        kst = place("kst", [P, KEYS], F32, at[0] - 4 * GW * 4)
        rs_at = at[0]
        rs = keep("rs", [P, 3, GW])
        nt = keep("nt", [P, 3, GW])
        probs = place("probs", [P, 2, T], F32, rs_at)
        act_lo = place("act_lo", [P, 2, T], F32R, rs_at)
        ident = keep("ident", [P, P])
        ones = keep("ones", [P, P])
        head_ones = keep("head_ones", [P, P])
        mod = keep("mod", [P, DEPTH * 48, 2])
        vecs = keep("vecs", [P, 80])
        lmod = keep("lmod", [P, 48, 2])
        lvec = keep("lvec", [P, 32])
        gs = keep("gs", [P, 2, DK, 2])
        silu_c = keep("silu_c", [P, 2, DK])
        chan_hi = keep("chan_hi", [P, 256], F32R)
        chan_lo = keep("chan_lo", [P, 256], F32R)
        cseq_hi = keep("cseq_hi", [P, 2, P], F32R)
        cseq_lo = keep("cseq_lo", [P, 2, P], F32R)
        eps_t = keep("eps_t", [P, 8])
        neg_max = keep("neg_max", [P, TILES])
        exp_sum = keep("exp_sum", [P, TILES])
        exp_inv = keep("exp_inv", [P, TILES])
        ph = at[0]

        def phase(first, *tensors):
            got, off = [], ph + first
            for name, shape, dt in tensors:
                got.append(place(name, shape, dt, off))
                off += int(np.prod(shape[1:])) * 4
            assert off <= room, (tensors[-1][0], off - room)
            return got

        h_hi, h_lo, act_hi = phase(0, ("h_hi", [P, DK, T], F32R), ("h_lo", [P, DK, T], F32R),
                                   ("act_hi", [P, 2, T], F32R))
        ev_p, = phase(2 * DK * T * 4, ("ev_p", [P, EV_SLOTS, GW], F32))
        EVB = EV_SLOTS * GW * 4
        ev_q, u_raw, u_hi, u_lo, a_hi, a_lo, r_raw, r_out = phase(
            0, ("ev_q", [P, EV_SLOTS, GW], F32), ("u_raw", [P, 2, T], F32), ("u_hi", [P, 2, T], F32R),
            ("u_lo", [P, 2, T], F32R), ("a_hi", [P, 9, 512], F32R), ("a_lo", [P, 9, 512], F32R),
            ("r_raw", [P, 2, 4, GW], F32), ("r_out", [P, RO_SLOTS, GW], F32))
        cache_t = place("cache_t", [P, 2, P], F32, rs_at + 3 * GW * 4)
        cq_raw, cq_hi, cq_lo, ckv_hi, ckv_lo, nat_out = phase(
            EVB, ("cq_raw", [P, 3, T], F32), ("cq_hi", [P, 3, T], F32R), ("cq_lo", [P, 3, T], F32R),
            ("ckv_hi", [P, 2, KEYS], F32R), ("ckv_lo", [P, 2, KEYS], F32R), ("nat_out", [P, 416], F32))
        cache_in, ctx_in = phase(EVB, ("cache_in", [P, 416], F32), ("ctx_in", [P, 4, P], F32))
        qst, vst, mq_hi, mq_lo, mk_hi, mk_lo, mv, gq2, gk2, gk_lo, gv2, pt_hi, pt_lo, o_bot, o_sum = phase(
            0, ("qst", [P, T], F32), ("vst", [P, KT, VD], F32), ("mq_hi", [P, T], F32R), ("mq_lo", [P, T], F32R),
            ("mk_hi", [P, KEYS], F32R), ("mk_lo", [P, KEYS], F32R), ("mv", [P, KT, P], F32R),
            ("gq2", [P, T], F32R), ("gk2", [P, KEYS], F32R), ("gk_lo", [P, KEYS], F32R), ("gv2", [P, KT, P], F32R),
            ("pt_hi", [P, 2, 9, 256], F32R), ("pt_lo", [P, 2, 9, 256], F32R),
            ("o_bot", [P, 256], F32), ("o_sum", [P, 256], F32))
        ADA_SLOTS = 4
        ada_w, vec_rows, ada_rows, c_in, tab_in, x_in = phase(
            0, ("ada_w", [P, ADA_SLOTS, DK, 512], F32), ("vec_rows", [80, P], F32), ("ada_rows", [96, P], F32),
            ("b_ada_t", [P, 96], F32), ("tab_in", [P, 512], F32), ("x_in", [P, 2, D_MODEL], F32))
        b_ada_t = c_in
        y_out, = phase(0, ("y_out", [P, 2, D_MODEL], F32))

        ps = ctx.enter_context(nc.psum_tensor("ps", [P, 8, 512], F32))

        def dram(name, shape):
            return nc.dram_tensor(name, shape, F32, kind="Internal").ap()

        s_in = dram("s_in", (SCR_ROWS, T))
        s_cq = dram("s_cq", (QR, T))
        s_qn = dram("s_qn", (HEADS, NOPE, T))
        s_qr = dram("s_qr", (7 * ROPE, T))
        s_qrr = dram("s_qrr", (HEADS, ROPE, T))
        s_kn = dram("s_kn", (HEADS, NOPE, KEYS))
        s_kr = dram("s_kr", (ROPE, KEYS))
        s_gq = dram("s_gq", (HEADS, VD, T))
        s_gk = dram("s_gk", (2, VD, KEYS))
        s_v = dram("s_v", (KEYS, 8, VD))
        s_cc = dram("s_cc", (KVR, CTX))
        s_mix = dram("s_mix", (16, 64, T))

        def sem(name):
            return ctx.enter_context(nc.semaphore(name))

        unit_loaded = [sem(f"unit_loaded{i}") for i in range(STAGES)]
        unit_hi = sem("unit_hi")
        unit_split = sem("unit_split")
        dft_used = sem("dft_used")
        ev_mm, ev_done = sem("ev_mm"), sem("ev_done")
        ev_stored = [sem(f"ev_stored{i}") for i in range(EV_SLOTS)]
        lay_ready, sq_used = sem("lay_ready"), sem("sq_used")
        sq_done, stat_mm, stat_y0 = sem("sq_done"), sem("stat_mm"), sem("stat_y0")
        newt_a, newt_b, stat_rs = sem("newt_a"), sem("newt_b"), sem("stat_rs")
        nx_mul, nx_mod, nx_hi, nx_done = sem("nx_mul"), sem("nx_mod"), sem("nx_hi"), sem("nx_done")
        u_loaded, u_split = sem("u_loaded"), sem("u_split")
        ch_mm, ch_hi, ch_lo = sem("ch_mm"), sem("ch_hi"), sem("ch_lo")
        r_loaded = [sem(f"r_loaded{i}") for i in range(2)]
        r_sq, r_dve, r_use = sem("r_sq"), sem("r_dve"), sem("r_use")
        r_stored = [sem(f"r_stored{i}") for i in range(RO_SLOTS)]
        dve_step = sem("dve_step")
        cq_loaded, cq_split, ckv_split = sem("cq_loaded"), sem("cq_split"), sem("ckv_split")
        cache_loaded, cache_stored, ctx_loaded, nat_stored = (
            sem("cache_loaded"), sem("cache_stored"), sem("ctx_loaded"), sem("nat_stored"))
        gv_copied = sem("gv_copied")
        tr_mm, tr_ev = sem("tr_mm"), sem("tr_ev")
        q_loaded, k_loaded, v_loaded = sem("q_loaded"), sem("k_loaded"), sem("v_loaded")
        prep_hi, prep_q, prep_k, prep_v = sem("prep_hi"), sem("prep_q"), sem("prep_k"), sem("prep_v")
        s_mm, max_done, exp_done, inv_done, p_done = (
            sem("s_mm"), sem("max_done"), sem("exp_done"), sem("inv_done"), sem("p_done"))
        t_mm, pt_hi_done, pt_lo_done = sem("t_mm"), sem("pt_hi_done"), sem("pt_lo_done")
        pv_mm, bot_done, o_done, o_stored = sem("pv_mm"), sem("bot_done"), sem("o_done"), sem("o_stored")
        mix_loaded = [sem(f"mix_loaded{i}") for i in range(4)]
        mix_hi, mix_split = sem("mix_hi"), sem("mix_split")
        out_mm, out_add = sem("out_mm"), sem("out_add")
        gate_mm, up_mm, silu_done, act_f, act_h, act_done = (
            sem("gate_mm"), sem("up_mm"), sem("silu_done"), sem("act_f"), sem("act_h"), sem("act_done"))
        down_mm, down_add = sem("down_mm"), sem("down_add")
        pre_loaded, pre_const, pre_ident, pre_tr, pre_vec, pre_silu, pre_tab = (
            sem("pre_loaded"), sem("pre_const"), sem("pre_ident"), sem("pre_tr"), sem("pre_vec"), sem("pre_silu"),
            sem("pre_tab"))
        x_loaded = [sem(f"x_loaded{i}") for i in range(2)]
        x_tr, x_ev_act, x_ev_dve = sem("x_tr"), sem("x_ev_act"), sem("x_ev_dve")
        ada_loaded = [sem(f"ada_loaded{i}") for i in range(ADA_SLOTS)]
        ada_mm, ada_ev = sem("ada_mm"), sem("ada_ev")
        y_mod, y_tr, y_ev_act, y_ev_dve = sem("y_mod"), sem("y_tr"), sem("y_ev_act"), sem("y_ev_dve")
        y_stored = [sem(f"y_stored{i}") for i in range(2)]

        w_in_v = a["w_in"].rearrange("l (k p) n -> l p k n", p=P)
        w_q_up_v = a["w_q_up"].rearrange("l (k p) (h n) -> l k p h n", p=P, h=HEADS)
        w_kv_up_v = a["w_kv_up"].rearrange("l (k p) (h c n) -> l k c p h n", p=P, h=HEADS, c=2)
        w_out_v = a["w_out"].rearrange("l (k p) n -> l p k n", p=P)
        w_gate_v = a["w_ffn_gate"].rearrange("l (k p) (c t n) -> l c t p k n", p=P, t=2, n=P)
        w_up_v = a["w_ffn_up"].rearrange("l (k p) (c t n) -> l c t p k n", p=P, t=2, n=P)
        w_down_v = a["w_ffn_down"].rearrange("l (c k p) (h n) -> l c h p k n", k=2, p=P, h=2)
        w_ada_v = a["w_ada"].rearrange("l (k p) (q n) -> l q p k n", p=P, n=512)
        mix_v = s_mix.rearrange("h r t -> (h r) t")

        def cols(g):
            return slice(g * GW, (g + 1) * GW)

        def key_pieces(g):
            if g == 0:
                return [(0, CTX, 0), (CTX, GW, CTX + PAST)]
            return [(0, GW, g * GW + PAST)]

        def halves(g):
            return [(0, 0, CTX), (1, CTX, GW)] if g == 0 else [(1, g * GW, (g + 1) * GW)]

        ps_flat = ps.rearrange("p b n -> p (b n)")

        def s_place(s):
            return ps_flat[:, 1536 * (s % 2):1536 * (s % 2) + T]

        def t_place(r, c):
            return [(3 * ((r + 1) % 2) + 2, P), (6, 0), (7, 256)][c]

        def unit_width(u):
            if u < U_DFT:
                return DK * IN_TILES[u][2]
            if U_QUP <= u < U_KVUP:
                return HEADS * (NOPE + ROPE)
            if U_KVUP <= u < U_OUT:
                return HEADS * (NOPE + VD)
            return 1024

        def wtiles(u, n):
            s = u % RING
            w = unit_width(u) if u < U_FFN else 1024
            return [t[:, s, 0:w].rearrange("p (k n) -> p k n", n=n) for t in (w_hi, w_lo)]

        block = ctx.enter_context(nc.Block())

        settled = {nc.sync: sem("settled_sp"), nc.gpsimd: sem("settled_pool"), nc.tensor: sem("settled_pe")}

        def settle(eng):
            eng.sem_inc(settled[eng], 1)

        @block.sync
        def _(sp):
            n = 0
            for src, r0, rn in (("c_ctx", 0, 8), ("c", 8, 8)):
                v = a[src] if src == "c_ctx" else a[src].rearrange("a d -> (a d)")
                sp.dma_start(vec_rows[r0:r0 + rn, :], v.rearrange("(k p) -> k p", p=P)).then_inc(pre_loaded, 16)
            sp.dma_start(vec_rows[16:32, :], a["g_norm1"].rearrange("l (k p) -> (l k) p", p=P)).then_inc(pre_loaded, 16)
            sp.dma_start(vec_rows[32:48, :], a["g_norm2"].rearrange("l (k p) -> (l k) p", p=P)).then_inc(pre_loaded, 16)
            sp.dma_start(vec_rows[48:56, :], a["g_final"].rearrange("(k p) -> k p", p=P)).then_inc(pre_loaded, 16)
            sp.dma_start(vec_rows[56:62, :], a["g_q_a"].rearrange("l (k p) -> (l k) p", p=P)).then_inc(pre_loaded, 16)
            sp.dma_start(vec_rows[62:66, :], a["g_kv_a"].rearrange("l (k p) -> (l k) p", p=P)).then_inc(pre_loaded, 16)
            for j, name in enumerate(("g_q_head", "g_k_head")):
                r0 = 66 + 2 * j
                sp.dma_start(vec_rows[r0:r0 + 2, 0:64], a[name]).then_inc(pre_loaded, 16)
                sp.dma_start(vec_rows[r0:r0 + 2, 64:128], a[name]).then_inc(pre_loaded, 16)
                for q in range(4):
                    sp.dma_start(vec_rows[r0 + 4:r0 + 6, 32 * q:32 * q + 32],
                                 a[name][:, 32 * (1 - q % 2):32 * (1 - q % 2) + 32]).then_inc(pre_loaded, 16)
            sp.dma_start(ada_rows[:, :], a["b_ada"].rearrange("l (k p) -> (l k) p", p=P)).then_inc(pre_loaded, 16)
            sp.dma_start(tab_in[:, 0:256], a["t_chan"]).then_inc(pre_loaded, 16)
            sp.dma_start(tab_in[:, 256:512], a["t_ctx"]).then_inc(pre_loaded, 16)
            for i in range(9):
                if i >= 2:
                    sp.wait_ge(x_tr, 2 * (i - 1))
                src = a["x_prompt"][0] if i == 0 else a["x_sample"][0, (i - 1) * P:i * P, :]
                sp.dma_start(x_in[:, i % 2, :], src).then_inc(x_loaded[i % 2], 16)
            for l in range(DEPTH):
                for q in range(12):
                    n = 12 * l + q
                    if n >= ADA_SLOTS:
                        sp.wait_ge(ada_mm, n - ADA_SLOTS + 1)
                    sp.dma_start(ada_w[:, n % ADA_SLOTS, :, :], w_ada_v[l, q]).then_inc(ada_loaded[n % ADA_SLOTS], 16)

            with sp.Fori(0, DEPTH) as l:
                def load_unit(u, src, dst_shape=None, c0=0, c1=None):
                    s = u % STAGES
                    sp.wait_ge(unit_split, l * UNITS + u + 1)
                    settle(sp)
                    dst = w_in_st[:, s, c0:c1 or unit_width(u)]
                    if dst_shape:
                        dst = dst.rearrange("p (k n) -> p k n", n=dst_shape)
                    sp.dma_start(dst, src).then_inc(unit_loaded[s], 16)

                def wait_ev_stored(jobs):
                    need = {}
                    for e in jobs:
                        need[e % EV_SLOTS] = max(need.get(e % EV_SLOTS, 0), EV_AFTER[e])
                    for s, v in sorted(need.items()):
                        sp.wait_ge(ev_stored[s], l * EV_TOTAL[s] + v)
                        settle(sp)

                def wait_ro_stored(uses):
                    need = {}
                    for e in uses:
                        need[e % RO_SLOTS] = max(need.get(e % RO_SLOTS, 0), RO_AFTER[e])
                    for s, v in sorted(need.items()):
                        sp.wait_ge(r_stored[s], l * RO_TOTAL[s] + v)
                        settle(sp)

                def load_r(r):
                    kind, t, g = R_JOBS[r]
                    s = r % 2
                    if r >= 2:
                        sp.wait_ge(r_dve, l * len(R_JOBS) + r - 1)
                        settle(sp)

                    def get(dst, src):
                        sp.dma_start(dst, src).then_inc(r_loaded[s], 16)

                    if kind in ("cq", "ckv"):
                        if g == 0:
                            first = [x_[0] for x_ in IN_TILES].index(kind)
                            wait_ev_stored(range(G * first, G * (first + (3 if kind == "cq" else 2))))
                        k = 3 if kind == "cq" else 2
                        rows = s_in[ROW[kind]:ROW[kind] + k * P, cols(g)]
                        get(r_raw[:, s, 0:k, :], rows.rearrange("(k p) t -> p k t", p=P))
                    elif kind in ("gk", "gq"):
                        u = [x_[0] for x_ in IN_TILES].index(kind) + t
                        wait_ev_stored([G * u + g])
                        r0 = ROW[kind] + t * P
                        get(r_raw[:, s, 0, :], s_in[r0:r0 + P, cols(g)])
                        for q in range(4):
                            q2 = q ^ 1
                            get(r_raw[32 * q:32 * q + 32, s, 1, :], s_in[r0 + 32 * q2:r0 + 32 * q2 + 32, cols(g)])
                        get(r_raw[:, s, 2:4, :], a["t_rope_gqa"][:, :, cols(g)])
                    else:
                        wait_ev_stored([E_QUP + 5 * g + 3 + t] + ([G * 7 + g] if t else []))
                        r0, n = (0, 8) if t == 0 else (P, 6)
                        get(r_raw[0:16 * n, s, 0, :], s_qr[r0:r0 + 16 * n, cols(g)])
                        for q in range(n):
                            q2 = q ^ 1
                            get(r_raw[16 * q:16 * q + 16, s, 1, :], s_qr[r0 + 16 * q2:r0 + 16 * q2 + 16, cols(g)])
                        get(r_raw[:, s, 2:4, :], a["t_rope_mla"][:, :, cols(g)])

                for u, (_, c0, w) in enumerate(IN_TILES):
                    load_unit(u, w_in_v[l, :, :, c0:c0 + w], w)
                sp.dma_start(s_v[CTX:CTX + PAST, HEADS:8, :], a["cache_gqa_v"][0, l]).then_inc(gv_copied, 16)

                def load_dft(i):
                    load_unit(U_DFT + i, a["t_seq"][i // 2, :, i % 2, :])

                for i in range(STAGES):
                    load_dft(i)
                wait_ev_stored(range(0, 2 * G))
                sp.wait_ge(ev_mm, l * EVJ + E_DFT)
                sp.dma_start(u_raw[:, :, :], s_in[0:256, :].rearrange("(k p) t -> p k t", p=P)).then_inc(u_loaded, 16)
                wait_ev_stored(range(E_DFT - EV_SLOTS, E_DFT))
                load_r(0)
                load_r(1)
                for i in range(STAGES, N_DFT):
                    load_dft(i)
                    if i - 1 < R_DFT:
                        load_r(i - 1)
                for r in range(N_DFT - 1, R_DFT):
                    load_r(r)
                for k in range(N_QUP):
                    load_unit(U_QUP + k, w_q_up_v[l, k, :, :, 0:NOPE], NOPE, 0, HEADS * NOPE)
                    sp.dma_start(w_in_st[:, (U_QUP + k) % STAGES, HEADS * NOPE:HEADS * (NOPE + ROPE)]
                                 .rearrange("p (h n) -> p h n", n=ROPE), w_q_up_v[l, k, :, :, NOPE:])\
                        .then_inc(unit_loaded[(U_QUP + k) % STAGES], 16)
                wait_ro_stored([n for n, (r, _, _) in enumerate(R_USES) if R_JOBS[r][0] == "cq"])
                sp.wait_ge(ch_mm, l * 9 + 9)
                sp.dma_start(cq_raw[:, :, :], s_cq.rearrange("(k p) t -> p k t", p=P)).then_inc(cq_loaded, 16)
                for k in range(N_KVUP):
                    load_unit(U_KVUP + k, w_kv_up_v[l, k, 0], NOPE, 0, HEADS * NOPE)
                    sp.dma_start(w_in_st[:, (U_KVUP + k) % STAGES, HEADS * NOPE:HEADS * (NOPE + VD)]
                                 .rearrange("p (h n) -> p h n", n=VD), w_kv_up_v[l, k, 1])\
                        .then_inc(unit_loaded[(U_KVUP + k) % STAGES], 16)
                for r in range(R_DFT, R_NORMED):
                    load_r(r)
                sp.wait_ge(cq_split, l * G + G)
                sp.dma_start(cache_in[:, 0:256], a["cache_mla_ckv"][0, l]).then_inc(cache_loaded, 16)
                sp.dma_start(cache_in[:, 256:288], a["cache_mla_krope"][0, l]).then_inc(cache_loaded, 16)
                sp.dma_start(cache_in[:, 288:416], a["cache_gqa_k"][0, l].rearrange("t h d -> t (h d)"))\
                    .then_inc(cache_loaded, 16)
                for r in range(R_NORMED, len(R_JOBS)):
                    load_r(r)
                for m in range(4):
                    load_unit(U_OUT + m, w_out_v[l, :, :, m * P:(m + 1) * P], P)
                sp.wait_ge(tr_ev, l * 8 + 4)
                sp.dma_start(s_gk[:, :, CTX:CTX + PAST].rearrange("h r t -> (h r) t"), cache_t[:, 1, :])\
                    .then_inc(cache_stored, 16)
                sp.dma_start(s_kr[:, CTX:CTX + PAST], cache_t[0:ROPE, 0, :]).then_inc(cache_stored, 16)
                wait_ro_stored(range(len(R_USES)))
                sp.dma_start(ctx_in[:, 0:2, :], s_cc.rearrange("(k p) t -> p k t", p=P)).then_inc(ctx_loaded, 16)
                sp.dma_start(ctx_in[0:ROPE, 2, :], s_kr[:, 0:CTX]).then_inc(ctx_loaded, 16)
                sp.dma_start(ctx_in[:, 3, :], s_gk[:, :, 0:CTX].rearrange("h r t -> (h r) t"))\
                    .then_inc(ctx_loaded, 16)
                sp.wait_ge(tr_ev, l * 8 + 8)
                sp.dma_start(o["new_mla_ckv"][0, l], nat_out[:, 0:256]).then_inc(nat_stored, 16)
                sp.dma_start(o["new_mla_krope"][0, l], nat_out[:, 256:288]).then_inc(nat_stored, 16)
                sp.dma_start(o["new_gqa_k"][0, l].rearrange("t h d -> t (h d)"), nat_out[:, 288:416])\
                    .then_inc(nat_stored, 16)
                wait_ev_stored(range(EVJ - EV_SLOTS, EVJ))
                sp.wait_ge(cache_stored, (l + 1) * 32)
                settle(sp)
                sp.wait_ge(gv_copied, (l + 1) * 16)
                settle(sp)
                sp.wait_ge(nat_stored, (l + 1) * 48)
                settle(sp)

                def load_mla(p, y):
                    sp.wait_ge(prep_q, y)
                    sp.dma_start(qst[0:NOPE, :], s_qn[p]).then_inc(q_loaded, 16)
                    sp.dma_start(qst[NOPE:96, :], s_qrr[p]).then_inc(q_loaded, 16)
                    sp.wait_ge(prep_k, y)
                    sp.dma_start(kst[0:NOPE, :], s_kn[p]).then_inc(k_loaded, 16)
                    sp.dma_start(kst[NOPE:96, :], s_kr).then_inc(k_loaded, 16)
                    sp.wait_ge(prep_v, y)
                    sp.dma_start(vst[:, :, :], s_v.rearrange("(k q) h d -> h q k d", q=P)[p]).then_inc(v_loaded, 16)

                def load_gqa(p, kv, y):
                    sp.wait_ge(prep_q, y)
                    for half in range(2):
                        sp.dma_start(qst[64 * half:64 * half + 64, :], s_gq[p]).then_inc(q_loaded, 16)
                    sp.wait_ge(prep_k, y)
                    for half in range(2):
                        sp.dma_start(kst[64 * half:64 * half + 64, :], s_gk[kv]).then_inc(k_loaded, 16)
                    sp.wait_ge(prep_v, y)
                    sp.dma_start(vst[:, :, :], s_v.rearrange("(k q) h d -> h q k d", q=P)[HEADS + kv])\
                        .then_inc(v_loaded, 16)

                def store_o(p, pi, g):
                    sp.wait_ge(o_done, pi * GROUPS + g + 1)
                    settle(sp)
                    row = p if g < 5 else 10 + p
                    c0, n = (0, CTX) if g % 5 == 4 else (CTX + 256 * (g % 5), 256)
                    sp.dma_start(s_mix[row, :, c0:c0 + n], o_sum[0:64, 0:n]).then_inc(o_stored, 16)

                load_mla(0, l * 12)

                def pair(p, kv, last=False):
                    pi = l * PAIRS + p
                    load_gqa(p, kv, pi * 2 + 1)
                    for g in range(3):
                        store_o(p, pi, g)
                    if not last:
                        load_mla(p + 1, pi * 2 + 2)
                    for g in range(3, GROUPS):
                        store_o(p, pi, g)

                with sp.Fori(0, 3) as p:
                    pair(p, 0)
                with sp.Fori(3, 5) as p:
                    pair(p, 1)
                pair(5, 1, last=True)

                sp.wait_ge(o_stored, (l + 1) * PAIRS * GROUPS * 16)
                for i in range(G * DK):
                    g, k = divmod(i, DK)
                    if i >= 4:
                        sp.wait_ge(mix_split, l * G * DK + i - 3)
                    sp.dma_start(wk[:, i % 4, :], mix_v[k * P:(k + 1) * P, cols(g)]).then_inc(mix_loaded[i % 4], 16)
                for m in range(4, N_OUT):
                    load_unit(U_OUT + m, w_out_v[l, :, :, m * P:(m + 1) * P], P)
                with sp.Fori(0, CHUNKS) as c:
                    for j in range(6):
                        s = (U_FFN + j) % STAGES
                        sp.wait_ge(unit_split, l * UNITS + c * 6 + U_FFN + j + 1)
                        if j < 4:
                            src = (w_gate_v, w_up_v)[j % 2][l, c, j // 2]
                            dst = w_in_st[:, s, :].rearrange("p (k n) -> p k n", n=P)
                        else:
                            src = w_down_v[l, c, j - 4]
                            dst = w_in_st[:, s, :].rearrange("p (k n) -> p k n", n=512)
                        sp.dma_start(dst, src).then_inc(unit_loaded[s], 16)

            for i in range(9):
                sp.wait_ge(y_ev_act, i + 1)
                sp.wait_ge(y_ev_dve, i + 1)
                dst = o["y_prompt"][0] if i == 0 else o["y_sample"][0, (i - 1) * P:i * P, :]
                sp.dma_start(dst, y_out[:, i % 2, :]).then_inc(y_stored[i % 2], 16)
            sp.wait_ge(y_stored[0], 5 * 16)
            sp.wait_ge(y_stored[1], 4 * 16)
            for s in range(EV_SLOTS):
                sp.wait_ge(ev_stored[s], DEPTH * EV_TOTAL[s])
            sp.wait_ge(nat_stored, DEPTH * 48)

        @block.gpsimd
        def _(pool):
            pool.memset(ident[:, :], 0.0).then_inc(pre_ident, 1)
            pool.wait_ge(pre_ident, 1)
            pool.affine_select(out=ident[:, :], in_=ident[:, :], compare_op=ALU.not_equal, fill=1.0, base=0,
                               pattern=[[-1, P]], channel_multiplier=1).then_inc(pre_ident, 1)

            with pool.Fori(0, DEPTH) as l:
                def wait_slot_used(u):
                    if u < 0:
                        pool.wait_ge(down_mm, l * (CHUNKS * G * DK))
                    elif u < U_DFT:
                        pool.wait_ge(ev_mm, l * EVJ + G * (u + 1))
                    elif u < U_QUP - 1:
                        pool.wait_ge(dft_used, l * (N_DFT - 1) + u - U_DFT + 1)
                    elif u < U_OUT:
                        pool.wait_ge(ev_mm, l * EVJ + (E_QUP if u < U_QUP else E_V if u < U_KVUP else EVJ))
                    else:
                        pool.wait_ge(out_mm, l * G * DK + G * (u - U_OUT + 1))

                def split_unit(u):
                    s, st, w = u % RING, u % STAGES, unit_width(u)
                    pool.wait_ge(unit_loaded[st], l * (STAGE_LOADS[st] * 16) + loads_through(u) * 16)
                    wait_slot_used(u - RING)
                    settle(pool)
                    pool.tensor_copy(w_hi[:, s, 0:w], w_in_st[:, st, 0:w]).then_inc(unit_hi, 1)
                    pool.wait_ge(unit_hi, l * UNITS + u + 1)
                    pool.tensor_tensor(w_lo[:, s, 0:w], w_in_st[:, st, 0:w], w_hi[:, s, 0:w].bitcast(F32),
                                       ALU.subtract).then_inc(unit_split, 1)

                def norm_mul(n0, stat0):
                    pool.wait_ge(sq_used, n0 + G * DK + 4)
                    for i in range(G * DK):
                        g, k = divmod(i, DK)
                        if k == 0:
                            pool.wait_ge(stat_rs, stat0 + g + 1)
                        if i >= 4:
                            pool.wait_ge(nx_done, n0 + i - 3)
                        pool.tensor_tensor(wk[:, i % 4, :], x[:, k, cols(g)], rs[:, g, :], ALU.mult)\
                            .then_inc(nx_mul, 1)

                for u in range(4):
                    split_unit(u)
                norm_mul(l * (2 * G * DK), l * STATS)
                for u in range(4, U_OUT + 4):
                    split_unit(u)

                def prep_steps(mla, pi, y):
                    pairs_done = pi * TILES + (9 if mla == "next" else 0)
                    groups_done = pi * GROUPS + (5 if mla == "next" else 0)
                    rows = 96 if mla else P
                    qh, kh, v2 = (mq_hi, mk_hi, mv) if mla else (gq2, gk2, gv2)

                    def q_high():
                        pool.wait_ge(q_loaded, (y + 1) * 32)
                        pool.wait_ge(s_mm, pairs_done)
                        settle(pool)
                        pool.tensor_copy(qh[0:rows, :], qst[0:rows, :]).then_inc(prep_hi, 1)

                    def q_low(tiles_done=0):
                        pool.wait_ge(prep_hi, y * 3 + 1)
                        if mla:
                            ins = pool.tensor_tensor(mq_lo[0:96, :], qst[0:96, :], mq_hi[0:96, :].bitcast(F32),
                                                     ALU.subtract)
                        else:
                            pool.wait_ge(p_done, tiles_done)
                            ins = pool.tensor_tensor(gq2[64:P, :], qst[64:P, :], gq2[64:P, :].bitcast(F32),
                                                     ALU.subtract)
                        ins.then_inc(prep_q, 1)

                    def k_high():
                        pool.wait_ge(k_loaded, (y + 1) * 32)
                        settle(pool)
                        pool.tensor_copy(kh[0:rows, :], kst[0:rows, :]).then_inc(prep_hi, 1)

                    def k_low():
                        pool.wait_ge(prep_hi, y * 3 + 2)
                        lo, n = (mk_lo, 96) if mla else (gk_lo, 64)
                        pool.tensor_tensor(lo[0:n, :], kst[0:n, :], kh[0:n, :].bitcast(F32), ALU.subtract)\
                            .then_inc(prep_k, 1)

                    def v_high():
                        pool.wait_ge(v_loaded, (y + 1) * 16)
                        pool.wait_ge(pv_mm, groups_done)
                        settle(pool)
                        pool.tensor_copy(v2[:, :, 0:VD], vst[:, :, :]).then_inc(prep_hi, 1)

                    def v_low():
                        pool.wait_ge(prep_hi, y * 3 + 3)
                        pool.tensor_tensor(v2[:, :, VD:P], vst[:, :, :], v2[:, :, 0:VD].bitcast(F32), ALU.subtract)\
                            .then_inc(prep_v, 1)

                    return [q_high, q_low, k_high, k_low, v_high, v_low]

                for step in prep_steps("first", l * PAIRS, l * 12):
                    step()

                def pair(p, last=False):
                    pi = l * PAIRS + p
                    steps = {0: prep_steps("", pi, pi * 2 + 1),
                             1: [] if last else prep_steps("next", pi, pi * 2 + 2)}
                    for s in range(TILES):
                        pool.wait_ge(inv_done, pi * TILES + s + 1)
                        settle(pool)
                        n = P if is_ctx(s) else T
                        pool.tensor_scalar(probs[:, s % 2, 0:n], probs[:, s % 2, 0:n], exp_inv[:, s:s + 1], 1.0,
                                           ALU.mult, ALU.mult).then_inc(p_done, 1)
                        todo = steps[s // 9]
                        if todo and s % 9 >= 1:
                            step = todo.pop(0)
                            if step.__name__ == "q_low":
                                step(pi * TILES + s + 1)
                                pool.wait_ge(prep_q, pi * 2 + (2 if s < 9 else 3))
                                settle(pool)
                            else:
                                step()
                    assert not steps[0] and not steps[1]

                with pool.Fori(0, 3) as p:
                    pair(p)
                with pool.Fori(3, 5) as p:
                    pair(p)
                pair(5, last=True)

                for u in range(U_OUT + 4, U_FFN + 4):
                    split_unit(u)
                norm_mul(l * (2 * G * DK) + G * DK, l * STATS + STATS - G)
                for u in range(U_FFN + 4, U_FFN + 6):
                    split_unit(u)
                with pool.Fori(1, CHUNKS) as c:
                    for j in range(6):
                        s, st = j, j % STAGES
                        n = l * UNITS + c * 6 + U_FFN + j
                        pool.wait_ge(unit_loaded[st], l * (STAGE_LOADS[st] * 16) + c * (6 // STAGES * 16)
                                     + loads_through(U_FFN + j) * 16)
                        if j < 4:
                            pool.wait_ge((gate_mm, up_mm)[j % 2], l * (CHUNKS * 6) + c * 6 - 6 + 3 * (j // 2 + 1))
                        else:
                            pool.wait_ge(down_mm, l * (CHUNKS * G * DK) + c * (G * DK) - 8 + 4 * (j - 3))
                        settle(pool)
                        pool.tensor_copy(w_hi[:, s, :], w_in_st[:, st, :]).then_inc(unit_hi, 1)
                        pool.wait_ge(unit_hi, n + 1)
                        pool.tensor_tensor(w_lo[:, s, :], w_in_st[:, st, :], w_hi[:, s, :].bitcast(F32),
                                           ALU.subtract).then_inc(unit_split, 1)

            for i in range(G * DK):
                g, k = divmod(i, DK)
                pool.wait_ge(sq_used, (2 * DEPTH + 1) * G * DK + 4)
                pool.wait_ge(stat_rs, DEPTH * STATS + g + 1)
                if i >= 4:
                    pool.wait_ge(y_mod, i - 3)
                pool.tensor_tensor(wk[:, i % 4, :], x[:, k, cols(g)], rs[:, g, :], ALU.mult).then_inc(nx_mul, 1)

        @block.scalar
        def _(act):
            act.wait_ge(pre_vec, 2)
            nc.scalar.activation(silu_c[:, :, :], vecs[:, 0:16].rearrange("p (c k) -> p c k", c=2), ACT.Silu)\
                .then_inc(pre_silu, 1)
            for i in range(9):
                act.wait_ge(x_tr, 2 * i + 1)
                nc.scalar.activation(x[:, 0:4, i * P:(i + 1) * P], ps[:, 0, :].rearrange("p (k t) -> p k t", k=4),
                                     ACT.Copy).then_inc(x_ev_act, 1)

            def root(stat, bank, dim):
                act.wait_ge(stat_rs, stat)
                nc.scalar.activation(nt[:, 0, :], ps[:, bank, 0:GW], ACT.Copy, bias=EPS, scale=1.0 / dim)
                nc.scalar.activation(nt[:, 1, :], ps[:, bank, 0:GW], ACT.Abs_reciprocal_sqrt, bias=eps_t[:, 0:1],
                                     scale=1.0 / dim).then_inc(stat_y0, 1)

            def norm_x(stat0, n0, which):
                for i in range(G * DK):
                    g, k = divmod(i, DK)
                    act.wait_ge(sq_used, n0 + i + 1)
                    nc.scalar.activation(wk[:, i % 4, :], x[:, k, cols(g)], ACT.Square).then_inc(sq_done, 1)
                for g in range(G):
                    act.wait_ge(sq_used, n0 + (g + 1) * DK + 4)
                    root(stat0 + g, 5 + g, D_MODEL)
                if which is None:
                    return
                for i in range(G * DK):
                    g, k = divmod(i, DK)
                    act.wait_ge(nx_mul, n0 + i + 1)
                    for c, c0, c1 in halves(g):
                        v = wk[:, i % 4, c0 - g * GW:c1 - g * GW]
                        ins = nc.scalar.activation(v, v, ACT.Identity, bias=lmod[:, 24 * which + k, c:c + 1],
                                                   scale=gs[:, which, k, c:c + 1])
                    ins.then_inc(nx_mod, 1)

            with act.Fori(0, DEPTH) as l:
                act.wait_ge(lay_ready, l + 1)
                norm_x(l * STATS, l * (2 * G * DK), 0)

                def store_ev(e, ev):
                    act.wait_ge(ev_done, l * EVJ + e + 1)
                    s = e % EV_SLOTS

                    def put(dst, src):
                        act.dma_start(dst, src).then_inc(ev_stored[s], 16)

                    if e < E_DFT:
                        u, g = divmod(e, G)
                        name, _, w = IN_TILES[u]
                        t = u - [x_[0] for x_ in IN_TILES].index(name)
                        if name == "kr":
                            put(s_qr[6 * ROPE:7 * ROPE, cols(g)], ev[0:ROPE, s, :])
                        elif name == "gv":
                            flat = s_v.rearrange("t h d -> t (h d)")[:, HEADS * VD:8 * VD]
                            if g == 0:
                                put(flat[0:CTX, :], ev[:, s, 0:P])
                                put(o["new_gqa_v"][0, l].rearrange("t h d -> t (h d)"), ev[:, s, 0:P])
                                put(flat[2 * P:4 * P, :].rearrange("(k q) d -> q k d", q=P),
                                    ev[:, s, P:3 * P].rearrange("q (k d) -> q k d", d=P))
                            else:
                                k0 = (3 * g + 1) * P
                                put(flat[k0:k0 + GW, :].rearrange("(k q) d -> q k d", q=P),
                                    ev[:, s, :].rearrange("q (k d) -> q k d", d=P))
                        else:
                            r0 = ROW[name] + t * P
                            put(s_in[r0:r0 + P, cols(g)], ev[:, s, :])
                    elif e == E_DFT:
                        put(mix_v[384:640, 0:CTX].rearrange("(f q) t -> q f t", q=P),
                            ev[:, s, 0:256].rearrange("q (f t) -> q f t", f=2))
                    elif e < E_QUP:
                        j = e - E_DFT - 1
                        r0, c0 = 384 + P * (j // 4), CTX + 256 * (j % 4)
                        put(mix_v[r0:r0 + P, c0:c0 + 256], ev[:, s, 0:256])
                    elif e < E_V:
                        g, mt = divmod(e - E_QUP, 5)
                        if mt < 3:
                            put(s_qn.rearrange("h r t -> (h r) t")[mt * P:(mt + 1) * P, cols(g)], ev[:, s, :])
                        else:
                            n = P if mt == 3 else 64
                            put(s_qr[(mt - 3) * P:(mt - 3) * P + n, cols(g)], ev[0:n, s, :])
                    elif e < E_K:
                        i = V_ORDER[e - E_V]
                        put(s_v.rearrange("t h d -> t (h d)")[i * P:(i + 1) * P, 0:HEADS * VD], ev[:, s, :])
                    else:
                        mt, kg = divmod(e - E_K, KG)
                        put(s_kn.rearrange("h r t -> (h r) t")[mt * P:(mt + 1) * P, kg * KGW:(kg + 1) * KGW],
                            ev[:, s, 0:KGW])

                def evacuate(e, ev, bank, rows, n, col=0, scale=1.0):
                    s = e % EV_SLOTS
                    act.wait_ge(ev_mm, l * EVJ + e + 1)
                    before = l * EV_TOTAL[s] + (EV_AFTER[e - EV_SLOTS] if e >= EV_SLOTS else 0)
                    act.wait_ge(ev_stored[s], before)
                    nc.scalar.activation(ev[0:rows, s, 0:n], ps[0:rows, bank, col:col + n], ACT.Copy, scale=scale)\
                        .then_inc(ev_done, 1)

                for e in range(E_DFT):
                    evacuate(e, ev_p, e % 6, IN_TILES[e // G][2], GW)
                    if e:
                        store_ev(e - 1, ev_p)
                store_ev(E_DFT - 1, ev_p)

                def r_squares(r):
                    kind, t, g = R_JOBS[r]
                    k = {"cq": 3, "ckv": 2}.get(kind, 1)
                    act.wait_ge(r_loaded[r % 2], l * RL_TOTAL[r % 2] + RL_AFTER[r])
                    act.wait_ge(stat_mm, l * R_NORMED + r)
                    nc.scalar.activation(wk[:, 0:k, :], r_raw[:, r % 2, 0:k, :], ACT.Square).then_inc(r_sq, 1)

                def r_root(r):
                    kind = R_JOBS[r][0]
                    act.wait_ge(stat_mm, l * R_NORMED + r + 1)
                    root(l * STATS + G + r, 4 + r % 2, {"cq": QR, "ckv": KVR}.get(kind, 64))

                def r_store(r):
                    kind, t, g = R_JOBS[r]
                    for n, (r_, i, k) in enumerate(R_USES):
                        if r_ != r or not k:
                            continue
                        s = n % RO_SLOTS
                        act.wait_ge(r_use, l * len(R_USES) + n + 1)

                        def put(dst, src):
                            act.dma_start(dst, src).then_inc(r_stored[s], 16)

                        if kind == "cq":
                            put(s_cq[i * P:(i + 1) * P, cols(g)], r_out[:, s, :])
                        elif kind == "gq":
                            put(s_gq.rearrange("h r t -> (h r) t")[t * P:(t + 1) * P, cols(g)], r_out[:, s, :])
                        elif kind == "gk":
                            for c0, c1, k0 in key_pieces(g):
                                put(s_gk.rearrange("h r t -> (h r) t")[:, k0:k0 + c1 - c0], r_out[:, s, c0:c1])
                        elif kind == "ckv":
                            put(s_cc[i * P:(i + 1) * P, :], r_out[:, s, 0:CTX])
                        elif t == 0:
                            put(s_qrr.rearrange("h r t -> (h r) t")[0:P, cols(g)], r_out[:, s, :])
                        else:
                            put(s_qrr.rearrange("h r t -> (h r) t")[P:6 * ROPE, cols(g)], r_out[0:64, s, :])
                            for c0, c1, k0 in key_pieces(g):
                                put(s_kr[:, k0:k0 + c1 - c0], r_out[64:96, s, c0:c1])

                for i in range(9):
                    act.wait_ge(ch_mm, l * 9 + i + 1)
                    nc.scalar.activation(a_hi[:, i, :], ps[:, i % 4, :], ACT.Copy).then_inc(ch_hi, 1)
                r_squares(0)
                evacuate(E_DFT, ev_q, 6, P, 256)
                store_ev(E_DFT, ev_q)
                for r in range(R_DFT):
                    r_root(r)
                    if r + 1 < R_DFT:
                        r_squares(r + 1)
                    r_store(r)
                for j in range(8):
                    evacuate(E_DFT + 1 + j, ev_q, j // 2, P, 256, col=256 * (j % 2))
                    store_ev(E_DFT + 1 + j, ev_q)
                for e in range(E_QUP, E_V):
                    g, mt = divmod(e - E_QUP, 5)
                    evacuate(e, ev_q, e % 4, 64 if mt == 4 else P, GW, scale=MLA_SCALE)
                    store_ev(e, ev_q)
                    if mt == 2:
                        r_squares(R_DFT + g)
                    if mt == 4:
                        r_root(R_DFT + g)
                        r_store(R_DFT + g)
                for e in range(E_V, EVJ):
                    evacuate(e, ev_q, e % 4, P, GW if e < E_K else KGW)
                    store_ev(e, ev_q)
                    if e == E_V + 6:
                        for r in range(R_NORMED, R_NORMED + 3):
                            r_store(r)
                for r in range(R_NORMED + 3, len(R_JOBS)):
                    r_store(r)

                def pair(p):
                    pi = l * PAIRS + p
                    for s in range(TILES + 3):
                        r = s - 2
                        if s - 3 in LAST_OF_GROUP:
                            g = LAST_OF_GROUP.index(s - 3)
                            n = CTX if g % 5 == 4 else 256
                            act.wait_ge(pv_mm, pi * GROUPS + g + 1)
                            act.wait_ge(o_done, pi * GROUPS + g)
                            nc.scalar.activation(o_bot[0:64, 0:n], ps[64:P, 7, 0:n], ACT.Copy).then_inc(bot_done, 1)
                        if 0 <= r < TILES:
                            b, q0 = group_of(r) % 2, P * ((r % 9) % 2)
                            for c, k0, n in chunks_of(r):
                                bank, col = t_place(r, c)
                                act.wait_ge(t_mm, pi * PAIR_CHUNKS + chunk_no(r, c) + 1)
                                if group_of(r) >= 2 and c == 0 and q0 == 0:
                                    act.wait_ge(pv_mm, pi * GROUPS + group_of(r) - 1)
                                nc.scalar.activation(pt_hi[:, b, k0:k0 + n, q0:q0 + P],
                                                     ps[:, bank, col:col + n * P].rearrange("p (k t) -> p k t", t=P),
                                                     ACT.Copy).then_inc(pt_hi_done, 1)
                        if s < TILES:
                            act.wait_ge(max_done, pi * TILES + s + 1)
                            if s >= 2:
                                act.wait_ge(t_mm, pi * PAIR_CHUNKS + chunks_through(s - 2))
                            n = P if is_ctx(s) else T
                            nc.scalar.activation(probs[:, s % 2, 0:n], s_place(s)[:, 0:n], ACT.Exp,
                                                 bias=neg_max[:, s:s + 1], accum_out=exp_sum[:, s:s + 1])\
                                .then_inc(exp_done, 1)

                with act.Fori(0, 5) as p:
                    pair(p)
                pair(5)

                act.wait_ge(out_add, (l + 1) * G * DK)
                norm_x(l * STATS + STATS - G, l * (2 * G * DK) + G * DK, 1)
                with act.Fori(0, CHUNKS) as c:
                    for j in range(6):
                        n = l * CHUNKS * 6 + c * 6 + j
                        g = j % 3
                        act.wait_ge(gate_mm, n + 1)
                        act.wait_ge(act_f, n + 1)
                        nc.scalar.activation(wk[:, j % 2, :], ps[:, 2 * g, 0:GW], ACT.Silu).then_inc(silu_done, 1)

            act.wait_ge(down_add, DEPTH * CHUNKS * G * DK + 6)
            norm_x(DEPTH * STATS, DEPTH * 2 * G * DK, None)
            for i in range(G * DK):
                g, k = divmod(i, DK)
                act.wait_ge(nx_mul, DEPTH * 2 * G * DK + i + 1)
                nc.scalar.activation(x[:, k, cols(g)], wk[:, i % 4, :], ACT.Copy, scale=vecs[:, 48 + k:49 + k])\
                    .then_inc(y_mod, 1)


            for i in range(9):
                act.wait_ge(y_tr, 2 * i + 1)
                if i >= 2:
                    act.wait_ge(y_stored[i % 2], i // 2 * 16)
                nc.scalar.activation(y_out[:, i % 2, 0:512], ps[:, 0, :], ACT.Copy).then_inc(y_ev_act, 1)

        @block.vector
        def _(dve):
            nc.vector.memset(ones[:, :], 1.0).then_inc(unit_split, STAGES)
            nc.vector.memset(head_ones[:, :], 0.0)
            nc.vector.memset(eps_t[:, 0:1], EPS).then_inc(sq_used, 4)
            nc.vector.memset(eps_t[:, 1:2], 0.0).then_inc(down_add, 6)
            nc.vector.memset(eps_t[:, 2:3], 0.0).then_inc(act_f, 2)
            dve.wait_ge(act_f, 2)
            for q in range(2):
                nc.vector.memset(head_ones[64 * q:64 * q + 64, 64 * q:64 * q + 64], 1.0).then_inc(pre_const, 1)
            dve.wait_ge(pre_tr, 1)
            nc.vector.tensor_copy(vecs[:, 0:74], ps[:, 4, 0:74]).then_inc(pre_vec, 1)
            nc.vector.tensor_copy(b_ada_t[:, :], ps[:, 4, 128:224]).then_inc(pre_vec, 1)
            nc.vector.tensor_copy(chan_hi[:, :], tab_in[:, 0:256]).then_inc(pre_tab, 1)
            nc.vector.tensor_copy(cseq_hi[:, :, :], tab_in[:, 256:512].rearrange("p (c t) -> p c t", c=2))\
                .then_inc(pre_tab, 1)
            dve.wait_ge(pre_tab, 2)
            nc.vector.tensor_tensor(chan_lo[:, :], tab_in[:, 0:256], chan_hi[:, :].bitcast(F32), ALU.subtract)\
                .then_inc(pre_tab, 1)
            nc.vector.tensor_tensor(cseq_lo[:, :, :], tab_in[:, 256:512].rearrange("p (c t) -> p c t", c=2),
                                    cseq_hi[:, :, :].bitcast(F32), ALU.subtract).then_inc(pre_tab, 1)
            for i in range(9):
                dve.wait_ge(x_tr, 2 * i + 2)
                nc.vector.tensor_copy(x[:, 4:8, i * P:(i + 1) * P], ps[:, 1, :].rearrange("p (k t) -> p k t", k=4))\
                    .then_inc(x_ev_dve, 1)
            dve.wait_ge(pre_vec, 2)
            mod_v = mod[:, :, :].rearrange("p (i s n) c -> p i s n c", s=ADA_SLOTS, n=4)
            b_v = b_ada_t[:, :].rearrange("p (i s n) -> p i s n", s=ADA_SLOTS, n=4)
            with dve.Fori(0, 24 // ADA_SLOTS) as i:
                for s in range(ADA_SLOTS):
                    dve.wait_ge(ada_mm, i * ADA_SLOTS + s + 1)
                    got = ps[:, 2 + s % 2, 0:8].rearrange("p (n c) -> p n c", c=2)
                    for c in range(2):
                        ins = nc.vector.tensor_tensor(mod_v[:, i, s, :, c], got[:, :, c], b_v[:, i, s, :], ALU.add)
                    ins.then_inc(ada_ev, 1)
            dve.wait_ge(ada_ev, 24)
            dve.wait_ge(x_ev_act, 9)
            dve.wait_ge(x_ev_dve, 9)

            def newton(stat, slot):
                dve.wait_ge(stat_y0, stat + 1)
                nc.vector.scalar_tensor_tensor(out=nt[:, 2, :], in0=nt[:, 1, :], scalar=-0.5, in1=nt[:, 1, :],
                                               op0=ALU.mult, op1=ALU.mult).then_inc(newt_a, 1)
                dve.wait_ge(newt_a, stat + 1)
                nc.vector.tensor_tensor(nt[:, 2, :], nt[:, 2, :], nt[:, 0, :], ALU.mult).then_inc(newt_b, 1)
                dve.wait_ge(newt_b, stat + 1)
                nc.vector.scalar_tensor_tensor(out=rs[:, slot, :], in0=nt[:, 2, :], scalar=1.5, in1=nt[:, 1, :],
                                               op0=ALU.add, op1=ALU.mult).then_inc(stat_rs, 1)

            def split_norm(n0):
                for i in range(G * DK):
                    g, k = divmod(i, DK)
                    dve.wait_ge(nx_mod, n0 + i + 1)
                    nc.vector.tensor_copy(h_hi[:, k, cols(g)], wk[:, i % 4, :]).then_inc(nx_hi, 1)
                    dve.wait_ge(nx_hi, n0 + i + 1)
                    nc.vector.tensor_tensor(h_lo[:, k, cols(g)], wk[:, i % 4, :], h_hi[:, k, cols(g)].bitcast(F32),
                                            ALU.subtract).then_inc(nx_done, 1)

            with dve.Fori(0, DEPTH) as l:
                steps = [0]

                def link(ins):
                    steps[0] += 1
                    ins.then_inc(dve_step, 1)
                    dve.wait_ge(dve_step, l * DVE_STEPS + steps[0])

                nc.vector.tensor_copy(lmod[:, :, :], mod[:, :, :].rearrange("p (l n) c -> p l n c", l=DEPTH)[:, l])
                nc.vector.tensor_copy(lvec[:, 0:3], vecs[:, 56:62].rearrange("p (l k) -> p l k", l=DEPTH)[:, l])
                nc.vector.tensor_copy(lvec[:, 3:5], vecs[:, 62:66].rearrange("p (l k) -> p l k", l=DEPTH)[:, l])
                nc.vector.tensor_copy(lvec[:, 5:9], vecs[:, 66:74].rearrange("p (v l) -> p l v", l=DEPTH)[:, l])
                nc.vector.tensor_copy(lvec[:, 9:17], vecs[:, 16:32].rearrange("p (l k) -> p l k", l=DEPTH)[:, l])
                link(nc.vector.tensor_copy(lvec[:, 17:25],
                                           vecs[:, 32:48].rearrange("p (l k) -> p l k", l=DEPTH)[:, l]))
                q_gains = lvec[:, 5:9].rearrange("p (a b) -> p a b", b=2)[:, :, 0]
                nc.vector.tensor_scalar(q_gains, q_gains, GQA_SCALE, None, ALU.mult)
                for which in range(2):
                    for c in range(2):
                        ins = nc.vector.scalar_tensor_tensor(
                            out=gs[:, which, :, c], in0=lmod[:, 24 * which + 8:24 * which + 16, c], scalar=1.0,
                            in1=lvec[:, 9 + 8 * which:17 + 8 * which], op0=ALU.add, op1=ALU.mult)
                ins.then_inc(lay_ready, 1)
                for g in range(G):
                    newton(l * STATS + g, g)
                split_norm(l * (2 * G * DK))

                dve.wait_ge(u_loaded, (l + 1) * 16)
                link(nc.vector.tensor_copy(u_hi[:, :, :], u_raw[:, :, :]))
                nc.vector.tensor_tensor(u_lo[:, :, :], u_raw[:, :, :], u_hi[:, :, :].bitcast(F32), ALU.subtract)\
                    .then_inc(u_split, 1)
                for i in range(9):
                    dve.wait_ge(ch_hi, l * 9 + i + 1)
                    nc.vector.tensor_tensor(a_lo[:, i, :], ps[:, i % 4, :], a_hi[:, i, :].bitcast(F32), ALU.subtract)\
                        .then_inc(ch_lo, 1)

                def r_job(r):
                    kind, t, g = R_JOBS[r]
                    s = r % 2
                    raw = r_raw[:, s]
                    if r < R_NORMED:
                        newton(l * STATS + G + r, r % 3)
                        dve.wait_ge(stat_rs, l * STATS + G + r + 1)
                    else:
                        dve.wait_ge(r_loaded[s], l * RL_TOTAL[s] + RL_AFTER[r])
                    for n, (r_, i, k) in enumerate(R_USES):
                        if r_ != r:
                            continue
                        slot = n % RO_SLOTS
                        out = r_out[:, slot, :]
                        dve.wait_ge(r_stored[slot], l * RO_TOTAL[slot] + (RO_AFTER[n - RO_SLOTS] if n >= RO_SLOTS else 0))
                        root_, last = rs[:, r % 3, :], None
                        if kind in ("cq", "ckv"):
                            gain = lvec[:, i:i + 1] if kind == "cq" else lvec[:, 3 + i:4 + i]
                            last = nc.vector.scalar_tensor_tensor(out=out, in0=raw[:, i, :], scalar=gain, in1=root_,
                                                                  op0=ALU.mult, op1=ALU.mult)
                            if kind == "ckv":
                                link(last)
                                last = None
                                for c0, c1, k0 in key_pieces(g):
                                    link(nc.vector.tensor_copy(ckv_hi[:, i, k0:k0 + c1 - c0], out[:, c0:c1]))
                                for c0, c1, k0 in key_pieces(g):
                                    k1 = k0 + c1 - c0
                                    ins = nc.vector.tensor_tensor(ckv_lo[:, i, k0:k1], out[:, c0:c1],
                                                                  ckv_hi[:, i, k0:k1].bitcast(F32), ALU.subtract)
                                ins.then_inc(r_use, 1)
                        elif kind in ("gk", "gq"):
                            v = 5 if kind == "gq" else 6
                            nc.vector.scalar_tensor_tensor(out=raw[:, 0, :], in0=raw[:, 0, :], scalar=lvec[:, v:v + 1],
                                                           in1=root_, op0=ALU.mult, op1=ALU.mult)
                            link(nc.vector.scalar_tensor_tensor(out=raw[:, 1, :], in0=raw[:, 1, :],
                                                                scalar=lvec[:, v + 2:v + 3], in1=root_,
                                                                op0=ALU.mult, op1=ALU.mult))
                        if kind in ("gk", "gq", "rope"):
                            m = 96 if kind == "rope" and t == 1 else P
                            nc.vector.tensor_tensor(raw[0:m, 0, :], raw[0:m, 0, :], raw[0:m, 2, :], ALU.mult)
                            link(nc.vector.tensor_tensor(raw[0:m, 1, :], raw[0:m, 1, :], raw[0:m, 3, :], ALU.mult))
                            last = nc.vector.tensor_tensor(out[0:m, :], raw[0:m, 0, :], raw[0:m, 1, :], ALU.add)
                        if last is not None:
                            last.then_inc(r_use, 1)
                    return last

                def r_end(r):
                    steps_of = [n for n, (r_, _, _) in enumerate(R_USES) if r_ == r]
                    dve.wait_ge(r_use, l * len(R_USES) + steps_of[-1] + 1)
                    nc.vector.memset(eps_t[:, 3:4], 0.0).then_inc(r_dve, 1)

                for r in range(R_DFT):
                    r_job(r)
                    r_end(r)
                dve.wait_ge(cq_loaded, (l + 1) * 16)
                link(nc.vector.tensor_copy(cq_hi[:, :, :], cq_raw[:, :, :]))
                dve.wait_ge(ev_mm, l * EVJ + E_QUP)
                for g in range(G):
                    nc.vector.tensor_tensor(cq_lo[:, :, cols(g)], cq_raw[:, :, cols(g)],
                                            cq_hi[:, :, cols(g)].bitcast(F32), ALU.subtract).then_inc(cq_split, 1)
                for r in range(R_DFT, R_NORMED):
                    r_job(r)
                    n = [n for n, (r_, _, _) in enumerate(R_USES) if r_ == r][-1]
                    dve.wait_ge(r_use, l * len(R_USES) + n + 1)
                    nc.vector.memset(eps_t[:, 3:4], 0.0).then_inc(r_dve, 1)
                    nc.vector.memset(eps_t[:, 4:5], 0.0).then_inc(ckv_split, 1)
                for i in range(2):
                    dve.wait_ge(tr_mm, l * 8 + i + 1)
                    link(nc.vector.tensor_copy(ckv_hi[:, i, CTX:CTX + PAST], ps[:, 6 + i, 0:P]))
                    nc.vector.tensor_tensor(ckv_lo[:, i, CTX:CTX + PAST], ps[:, 6 + i, 0:P],
                                            ckv_hi[:, i, CTX:CTX + PAST].bitcast(F32), ALU.subtract)\
                        .then_inc(tr_ev, 1)
                dve.wait_ge(tr_ev, l * 8 + 2)
                nc.vector.memset(eps_t[:, 4:5], 0.0).then_inc(ckv_split, 1)
                dve.wait_ge(tr_mm, l * 8 + 3)
                nc.vector.tensor_copy(cache_t[0:ROPE, 0, :], ps[0:ROPE, 6, 0:P]).then_inc(tr_ev, 1)
                dve.wait_ge(tr_mm, l * 8 + 4)
                nc.vector.tensor_copy(cache_t[:, 1, :], ps[:, 7, 0:P]).then_inc(tr_ev, 1)
                for r in range(R_NORMED, len(R_JOBS)):
                    r_job(r)
                    r_end(r)
                for i, (c0, w) in enumerate(((0, P), (P, P), (256, ROPE), (288, P))):
                    dve.wait_ge(tr_mm, l * 8 + 5 + i)
                    if i == 0:
                        dve.wait_ge(nat_stored, l * 48)
                    nc.vector.tensor_copy(nat_out[:, c0:c0 + w], ps[:, 6 + i % 2, 0:w]).then_inc(tr_ev, 1)

                def inverse(pi, s):
                    dve.wait_ge(exp_done, pi * TILES + s + 1)
                    nc.vector.reciprocal(exp_inv[:, s:s + 1], exp_sum[:, s:s + 1]).then_inc(inv_done, 1)

                def pair(p):
                    pi = l * PAIRS + p
                    for s in range(TILES + 3):
                        r = s - 2
                        if s < TILES:
                            dve.wait_ge(s_mm, pi * TILES + s + 1)
                            n = P if is_ctx(s) else T
                            nc.vector.tensor_reduce(neg_max[:, s:s + 1], s_place(s)[:, 0:n], AX_X, ALU.max,
                                                    negate=True).then_inc(max_done, 1)
                        if 1 <= s <= TILES:
                            inverse(pi, s - 1)
                        if s - 3 in LAST_OF_GROUP:
                            g = LAST_OF_GROUP.index(s - 3)
                            n = CTX if g % 5 == 4 else 256
                            dve.wait_ge(bot_done, pi * GROUPS + g + 1)
                            dve.wait_ge(o_stored, (pi * GROUPS + g) * 16)
                            nc.vector.tensor_tensor(o_sum[0:64, 0:n], ps[0:64, 7, 0:n], o_bot[0:64, 0:n], ALU.add)\
                                .then_inc(o_done, 1)
                        if 0 <= r < TILES:
                            b, q0 = group_of(r) % 2, P * ((r % 9) % 2)
                            for c, k0, n in chunks_of(r):
                                bank, col = t_place(r, c)
                                dve.wait_ge(pt_hi_done, pi * PAIR_CHUNKS + chunk_no(r, c) + 1)
                                nc.vector.tensor_tensor(
                                    pt_lo[:, b, k0:k0 + n, q0:q0 + P],
                                    ps[:, bank, col:col + n * P].rearrange("p (k t) -> p k t", t=P),
                                    pt_hi[:, b, k0:k0 + n, q0:q0 + P].bitcast(F32), ALU.subtract)\
                                    .then_inc(pt_lo_done, 1)

                with dve.Fori(0, 5) as p:
                    pair(p)
                pair(5)

                for i in range(G * DK):
                    g, k = divmod(i, DK)
                    dve.wait_ge(mix_loaded[i % 4], l * (G * DK // 4 * 16) + (i // 4 + 1) * 16)
                    nc.vector.tensor_copy(h_hi[:, k, cols(g)], wk[:, i % 4, :]).then_inc(mix_hi, 1)
                    dve.wait_ge(mix_hi, l * G * DK + i + 1)
                    nc.vector.tensor_tensor(h_lo[:, k, cols(g)], wk[:, i % 4, :], h_hi[:, k, cols(g)].bitcast(F32),
                                            ALU.subtract).then_inc(mix_split, 1)

                def add_gated(m, g, gate, bank, done):
                    for c, c0, c1 in halves(g):
                        ins = nc.vector.scalar_tensor_tensor(
                            out=x[:, m, c0:c1], in0=ps[:, bank, c0 - g * GW:c1 - g * GW],
                            scalar=lmod[:, gate + m, c:c + 1], in1=x[:, m, c0:c1], op0=ALU.mult, op1=ALU.add)
                    ins.then_inc(done, 1)

                for n in range(G * DK):
                    m, g = divmod(n, G)
                    dve.wait_ge(out_mm, l * G * DK + n + 1)
                    add_gated(m, g, 16, n % 6, out_add)
                for g in range(G):
                    newton(l * STATS + STATS - G + g, g)
                split_norm(l * (2 * G * DK) + G * DK)
                with dve.Fori(0, CHUNKS) as c:
                    for j in range(6):
                        t, g = divmod(j, G)
                        n = l * (CHUNKS * 6) + c * 6 + j
                        dve.wait_ge(silu_done, n + 1)
                        dve.wait_ge(up_mm, n + 1)
                        nc.vector.tensor_tensor(wk[:, 2 + j % 2, :], ps[:, 2 * g + 1, 0:GW], wk[:, j % 2, :], ALU.mult)\
                            .then_inc(act_f, 1)
                        dve.wait_ge(act_f, n + 3)
                        nc.vector.tensor_copy(act_hi[:, t, cols(g)], wk[:, 2 + j % 2, :]).then_inc(act_h, 1)
                        dve.wait_ge(act_h, n + 1)
                        nc.vector.tensor_tensor(act_lo[:, t, cols(g)], wk[:, 2 + j % 2, :],
                                                act_hi[:, t, cols(g)].bitcast(F32), ALU.subtract).then_inc(act_done, 1)
                    for d in range(G * DK):
                        g, m = divmod(d, DK)
                        dve.wait_ge(down_mm, l * (CHUNKS * G * DK) + c * (G * DK) + d + 1)
                        add_gated(m, g, 40, d % 6, down_add)
                dve.wait_ge(down_add, (l + 1) * (CHUNKS * G * DK) + 6)
                assert steps[0] == DVE_STEPS, steps[0]

            for g in range(G):
                newton(DEPTH * STATS + g, g)
            for i in range(9):
                dve.wait_ge(y_tr, 2 * i + 2)
                if i >= 2:
                    dve.wait_ge(y_stored[i % 2], i // 2 * 16)
                nc.vector.tensor_copy(y_out[:, i % 2, 512:1024], ps[:, 1, :]).then_inc(y_ev_dve, 1)

        @block.tensor
        def _(pe):
            def mm3(out, wh, wl, xh, xl, first, last):
                nc.tensor.matmul(out, wh, xh, start=first, stop=False)
                nc.tensor.matmul(out, wh, xl, start=False, stop=False)
                return nc.tensor.matmul(out, wl, xh, start=False, stop=last)

            pe.wait_ge(pre_ident, 2)
            pe.wait_ge(pre_const, 2)
            pe.wait_ge(pre_loaded, PRE_LOADS * 16)
            nc.tensor.transpose(ps[:, 4, 0:74], vec_rows[0:74, :], ident[0:74, 0:74])
            nc.tensor.transpose(ps[:, 4, 128:224], ada_rows[:, :], ident[0:96, 0:96]).then_inc(pre_tr, 1)
            for i in range(9):
                pe.wait_ge(x_loaded[i % 2], (i // 2 + 1) * 16)
                for half in range(2):
                    pe.wait_ge((x_ev_act, x_ev_dve)[half], i)
                    for j in range(4):
                        k = 4 * half + j
                        ins = nc.tensor.transpose(ps[:, half, j * P:(j + 1) * P], x_in[:, i % 2, k * P:(k + 1) * P],
                                                  ident[:, :])
                    ins.then_inc(x_tr, 1)
            pe.wait_ge(pre_silu, 1)
            with pe.Fori(0, 24 // ADA_SLOTS) as i:
                for s in range(ADA_SLOTS):
                    pe.wait_ge(ada_loaded[s], i * 16 + 16)
                    if s >= 2:
                        pe.wait_ge(ada_ev, i * ADA_SLOTS + s - 1)
                    else:
                        pe.wait_ge(ada_ev, i * ADA_SLOTS)
                    for j in range(4):
                        for k in range(DK):
                            ins = nc.tensor.matmul(ps[:, 2 + s % 2, 2 * j:2 * j + 2], ada_w[:, s, k, j * P:(j + 1) * P],
                                                   silu_c[:, :, k], start=(k == 0), stop=(k == DK - 1))
                    ins.then_inc(ada_mm, 1)

            def sum_squares(n0):
                for i in range(G * DK):
                    g, k = divmod(i, DK)
                    pe.wait_ge(sq_done, n0 + i + 1)
                    nc.tensor.matmul(ps[:, 5 + g, 0:GW], ones[:, :], wk[:, i % 4, :], start=(k == 0),
                                     stop=(k == DK - 1)).then_inc(sq_used, 1)

            with pe.Fori(0, DEPTH) as l:
                def unit(u, n):
                    pe.wait_ge(unit_split, l * UNITS + u + 1 + STAGES)
                    return wtiles(u, n)

                sum_squares(l * (2 * G * DK))
                for u, (name, _, w) in enumerate(IN_TILES):
                    wh, wl = unit(u, w)
                    for g in range(G):
                        e = G * u + g
                        if u == 0:
                            pe.wait_ge(nx_done, l * (2 * G * DK) + (g + 1) * DK)
                        if e >= 6:
                            pe.wait_ge(ev_done, l * EVJ + e - 5)
                        if name == "gv":
                            for i in range(3):
                                t0 = g * GW + i * P
                                out = ps[:, e % 6, i * P:(i + 1) * P]
                                for k in range(DK):
                                    ins = mm3(out, h_hi[:, k, t0:t0 + P], h_lo[:, k, t0:t0 + P], wh[:, k, :],
                                              wl[:, k, :], k == 0, k == DK - 1)
                        else:
                            for k in range(DK):
                                ins = mm3(ps[0:w, e % 6, 0:GW], wh[:, k, :], wl[:, k, :], h_hi[:, k, cols(g)],
                                          h_lo[:, k, cols(g)], k == 0, k == DK - 1)
                        ins.then_inc(ev_mm, 1)

                pe.wait_ge(u_split, l + 1)
                pe.wait_ge(ev_done, l * EVJ + E_DFT)
                pe.wait_ge(pre_tab, 4)
                for i in range(9):
                    if i >= 4:
                        pe.wait_ge(ch_lo, l * 9 + i - 3)
                    for f in range(2):
                        ts = slice(i * P, (i + 1) * P)
                        ins = mm3(ps[:, i % 4, 256 * f:256 * f + 256], u_hi[:, f, ts], u_lo[:, f, ts], chan_hi[:, :],
                                  chan_lo[:, :], True, True)
                    ins.then_inc(ch_mm, 1)
                pe.wait_ge(ch_lo, l * 9 + 9)

                def a_part(i, f, cs):
                    c0 = 256 * f + 128 * cs
                    return a_hi[:, i, c0:c0 + P], a_lo[:, i, c0:c0 + P]

                for f in range(2):
                    for cs in range(2):
                        ah, al = a_part(0, f, cs)
                        ins = mm3(ps[:, 6, P * f:P * f + P], ah, al, cseq_hi[:, cs, :], cseq_lo[:, cs, :],
                                  cs == 0, cs == 1)
                ins.then_inc(ev_mm, 1)

                def r_stat(r):
                    kind, t, g = R_JOBS[r]
                    k = {"cq": 3, "ckv": 2}.get(kind, 1)
                    pe.wait_ge(r_sq, l * R_NORMED + r + 1)
                    if r >= 2:
                        pe.wait_ge(stat_y0, l * STATS + G + r - 1)
                    for i in range(k):
                        ins = nc.tensor.matmul(ps[:, 4 + r % 2, 0:GW], (ones if k > 1 else head_ones)[:, :],
                                               wk[:, i, :], start=(i == 0), stop=(i == k - 1))
                    ins.then_inc(stat_mm, 1)

                for i in range(N_DFT):
                    wh, wl = unit(U_DFT + i, 512)
                    for f in range(2):
                        ah, al = a_part(1 + i // 2, f, i % 2)
                        for half in range(2):
                            ins = mm3(ps[:, 2 * f + half, :], ah, al, wh[:, half, :], wl[:, half, :],
                                      i == 0, i == N_DFT - 1)
                            if i == N_DFT - 1:
                                ins.then_inc(ev_mm, 2)
                    if i < N_DFT - 1:
                        ins.then_inc(dft_used, 1)
                    if i < R_DFT:
                        r_stat(i)

                uq = [unit(U_QUP + k, HEADS * (NOPE + ROPE)) for k in range(N_QUP)]
                for e in range(E_QUP, E_V):
                    g, mt = divmod(e - E_QUP, 5)
                    if mt == 0:
                        pe.wait_ge(cq_split, l * G + g + 1)
                    if e < E_QUP + 4:
                        pe.wait_ge(ev_done, l * EVJ + E_DFT + 1 + 2 * (e % 4 + 1))
                    else:
                        pe.wait_ge(ev_done, l * EVJ + e - 3)
                    m = 64 if mt == 4 else P
                    for k in range(N_QUP):
                        wh, wl = (t[:, 0, mt * P:mt * P + m] for t in uq[k])
                        ins = mm3(ps[0:m, e % 4, 0:GW], wh, wl, cq_hi[:, k, cols(g)], cq_lo[:, k, cols(g)],
                                  k == 0, k == N_QUP - 1)
                    ins.then_inc(ev_mm, 1)
                    if mt == 4:
                        r_stat(R_DFT + g)
                pe.wait_ge(cache_loaded, (l + 1) * 48)
                for i, (c0, w) in enumerate(((0, P), (P, P), (256, ROPE), (288, P))):
                    if i >= 2:
                        pe.wait_ge(tr_ev, l * 8 + i - 1)
                        settle(pe)
                    nc.tensor.transpose(ps[0:w, 6 + i % 2, 0:P], cache_in[:, c0:c0 + w], ident[:, :]).then_inc(tr_mm, 1)
                uk = [unit(U_KVUP + k, HEADS * (NOPE + VD)) for k in range(N_KVUP)]
                for e in range(E_V, EVJ):
                    pe.wait_ge(ev_done, l * EVJ + e - 3)
                    if e < E_K:
                        kt = V_ORDER[e - E_V]
                        pe.wait_ge(ckv_split, l * 4 + (4 if kt == 1 else 1 + max(kt - 1, 0) // 3))
                        ks = slice(kt * P, (kt + 1) * P)
                        for k in range(N_KVUP):
                            wh, wl = (t[:, 0, HEADS * NOPE:] for t in uk[k])
                            ins = mm3(ps[:, e % 4, 0:HEADS * VD], ckv_hi[:, k, ks], ckv_lo[:, k, ks], wh, wl,
                                      k == 0, k == N_KVUP - 1)
                    else:
                        mt, kg = divmod(e - E_K, KG)
                        ks = slice(kg * KGW, (kg + 1) * KGW)
                        for k in range(N_KVUP):
                            wh, wl = (t[:, 0, mt * P:(mt + 1) * P] for t in uk[k])
                            ins = mm3(ps[:, e % 4, 0:KGW], wh, wl, ckv_hi[:, k, ks], ckv_lo[:, k, ks],
                                      k == 0, k == N_KVUP - 1)
                    ins.then_inc(ev_mm, 1)
                pe.wait_ge(ctx_loaded, (l + 1) * 48)
                for i, w in enumerate((P, P, ROPE, P)):
                    pe.wait_ge(tr_ev, l * 8 + 3 + i)
                    settle(pe)
                    nc.tensor.transpose(ps[:, 6 + i % 2, 0:w], ctx_in[0:w, i, :], ident[0:w, 0:w]).then_inc(tr_mm, 1)
                pe.wait_ge(ev_done, (l + 1) * EVJ)
                pe.wait_ge(tr_ev, (l + 1) * 8)
                settle(pe)

                def pair(p):
                    pi = l * PAIRS + p
                    for s in range(TILES + 3):
                        mla = s < 9
                        if s < TILES:
                            t = s % 9
                            if t == 0:
                                y = pi * 2 + (0 if mla else 1)
                                pe.wait_ge(prep_q, y + 1)
                                pe.wait_ge(prep_k, y + 1)
                            if s >= 2:
                                pe.wait_ge(exp_done, pi * TILES + s - 1)
                            q0 = 0 if is_ctx(s) else CTX + t * P
                            qs = slice(q0, q0 + P)
                            parts = [(0, P, 0)] if is_ctx(s) else [(0, 512, CTX), (512, 512, CTX + 512),
                                                                   (1024, P, CTX + 1024)]
                            for c0, n, k0 in parts:
                                if c0 == 1024 and s >= 3:
                                    pe.wait_ge(pt_lo_done, pi * PAIR_CHUNKS + chunk_no(s - 3) + 1)
                                out, ks = s_place(s)[:, c0:c0 + n], slice(k0, k0 + n)
                                if mla:
                                    ins = mm3(out, mq_hi[0:96, qs], mq_lo[0:96, qs], mk_hi[0:96, ks], mk_lo[0:96, ks],
                                              True, True)
                                else:
                                    nc.tensor.matmul(out, gq2[:, qs], gk2[:, ks], start=True, stop=False)
                                    ins = nc.tensor.matmul(out, gq2[0:64, qs], gk_lo[0:64, ks], start=False, stop=True)
                            ins.then_inc(s_mm, 1)
                        if s - 3 in LAST_OF_GROUP:
                            g = LAST_OF_GROUP.index(s - 3)
                            if g % 5 == 0:
                                pe.wait_ge(prep_v, pi * 2 + (1 if g < 5 else 2))
                            pe.wait_ge(pt_lo_done, pi * PAIR_CHUNKS + chunks_through(s - 3))
                            pe.wait_ge(o_done, pi * GROUPS + g)
                            if 0 <= s - 3 < TILES - 0 and s - 3 + 1 < TILES and s >= 3:
                                pe.wait_ge(pt_lo_done, pi * PAIR_CHUNKS + chunks_through(s - 3))
                            v2 = mv if g < 5 else gv2
                            n, tiles_, kt0 = (CTX, 1, 0) if g % 5 == 4 else (256, 9, 1)
                            for kt in range(tiles_):
                                for part, pt in enumerate((pt_hi, pt_lo)):
                                    ins = nc.tensor.matmul(ps[:, 7, 0:n], v2[:, kt0 + kt, :], pt[:, g % 2, kt, 0:n],
                                                           start=(kt == 0 and part == 0),
                                                           stop=(kt == tiles_ - 1 and part == 1))
                            ins.then_inc(pv_mm, 1)
                        r = s - 2
                        if 0 <= r < TILES:
                            pe.wait_ge(p_done, pi * TILES + r + 1)
                            for c, k0, n in chunks_of(r):
                                bank, col = t_place(r, c)
                                if c == 0 and s - 1 < TILES:
                                    pe.wait_ge(exp_done, pi * TILES + s)
                                if c == 1 and r >= 1:
                                    pe.wait_ge(pt_lo_done, pi * PAIR_CHUNKS + chunks_through(r - 1))
                                if c == 2 and s - 3 in LAST_OF_GROUP:
                                    pe.wait_ge(o_done, pi * GROUPS + LAST_OF_GROUP.index(s - 3) + 1)
                                for j in range(n):
                                    kt = k0 + j
                                    ins = nc.tensor.transpose(ps[:, bank, col + j * P:col + (j + 1) * P],
                                                              probs[:, r % 2, kt * P:(kt + 1) * P], ident[:, :])
                                ins.then_inc(t_mm, 1)

                with pe.Fori(0, 5) as p:
                    pair(p)
                pair(5)

                for u in range(U_OUT, U_FFN):
                    m = u - U_OUT
                    wh, wl = unit(u, P)
                    for g in range(G):
                        n = m * G + g
                        if m == 0:
                            pe.wait_ge(mix_split, l * G * DK + (g + 1) * DK)
                        if n >= 6:
                            pe.wait_ge(out_add, l * G * DK + n - 5)
                        for k in range(DK):
                            ins = mm3(ps[:, n % 6, 0:GW], wh[:, k, :], wl[:, k, :], h_hi[:, k, cols(g)],
                                      h_lo[:, k, cols(g)], k == 0, k == DK - 1)
                        ins.then_inc(out_mm, 1)
                sum_squares(l * (2 * G * DK) + G * DK)
                pe.wait_ge(nx_done, (l + 1) * (2 * G * DK))
                settle(pe)
                with pe.Fori(0, CHUNKS) as c:
                    c6 = l * (CHUNKS * 6) + c * 6
                    c24 = l * (CHUNKS * G * DK) + c * (G * DK)

                    def ffn_unit(j, n):
                        pe.wait_ge(unit_split, l * UNITS + c * 6 + U_FFN + j + 1 + STAGES)
                        return wtiles(j, n) if j < 4 else wtiles(j, n)

                    for t in range(2):
                        gate, up = ffn_unit(2 * t, P), ffn_unit(2 * t + 1, P)
                        for g in range(G):
                            j = 3 * t + g
                            for b, (w, done) in enumerate(((gate, gate_mm), (up, up_mm))):
                                if t == 0:
                                    pe.wait_ge(down_add, c24 + 2 * g + b + 1)
                                elif b == 0:
                                    pe.wait_ge(silu_done, c6 + j - 2)
                                else:
                                    pe.wait_ge(act_f, c6 + j)
                                for k in range(DK):
                                    ins = mm3(ps[:, 2 * g + b, 0:GW], w[0][:, k, :], w[1][:, k, :], h_hi[:, k, cols(g)],
                                              h_lo[:, k, cols(g)], k == 0, k == DK - 1)
                                ins.then_inc(done, 1)
                    down = ffn_unit(4, 512), ffn_unit(5, 512)
                    for d in range(G * DK):
                        g, m = divmod(d, DK)
                        if m == 0:
                            pe.wait_ge(act_done, c6 + 3 + g + 1)
                        if d >= 6:
                            pe.wait_ge(down_add, c24 + d + 1)
                        elif d % 2 == 0:
                            pe.wait_ge(silu_done, c6 + 3 + d // 2 + 1)
                        else:
                            pe.wait_ge(act_f, c6 + 3 + d // 2 + 3)
                        wh, wl = down[m // 4]
                        m0 = (m % 4) * P
                        for t in range(2):
                            ins = mm3(ps[:, d % 6, 0:GW], wh[:, t, m0:m0 + P], wl[:, t, m0:m0 + P],
                                      act_hi[:, t, cols(g)], act_lo[:, t, cols(g)], t == 0, t == 1)
                        ins.then_inc(down_mm, 1)

            sum_squares(DEPTH * 2 * G * DK)
            for i in range(9):
                pe.wait_ge(y_mod, (i // 3 + 1) * DK)
                for half in range(2):
                    pe.wait_ge((y_ev_act, y_ev_dve)[half], i)
                    for j in range(4):
                        ins = nc.tensor.transpose(ps[:, half, j * P:(j + 1) * P],
                                                  x[:, 4 * half + j, i * P:(i + 1) * P], ident[:, :])
                    ins.then_inc(y_tr, 1)


def tables():
    def dft(n, sign):
        k = np.arange(n)
        ang = 2 * np.pi * (np.outer(k, k) % n) / n
        return np.cos(ang), sign * np.sin(ang)

    c64, s64 = dft(64, 1.0)
    chan = np.zeros((P, 2, P))
    for i, t in enumerate((c64, s64)):
        for b in range(2):
            chan[64 * b:64 * b + 64, i, 64 * b:64 * b + 64] = t / 8.0
    c, s = dft(CTX, -1.0)
    t_ctx = np.stack([c, s], axis=1) / np.sqrt(CTX)
    c, s = dft(LAT, -1.0)
    t_seq = np.stack([c, s], axis=1).reshape(LAT // P, P, 2, LAT) / 32.0

    def rope(dim, copies):
        f = np.float32
        n_axis = dim // 4
        inv = (f(10000.0) ** (-np.arange(n_axis, dtype=f) / f(n_axis))).astype(f)
        t = np.arange(LAT)
        ang = np.concatenate([(t // GRID_W).astype(f)[:, None] * inv, (t % GRID_W).astype(f)[:, None] * inv], axis=1)
        cos, sin = np.cos(ang.astype(np.float64)).T, np.sin(ang.astype(np.float64)).T
        out = np.zeros((P, 2, T))
        out[:, 0, :CTX] = 1.0
        out[:, 0, CTX:] = np.tile(np.concatenate([cos, cos]), (copies, 1))
        out[:, 1, CTX:] = np.tile(np.concatenate([-sin, sin]), (copies, 1))
        return out

    f = {"t_chan": chan.reshape(P, 256), "t_ctx": t_ctx.reshape(P, 256), "t_seq": t_seq,
         "t_rope_gqa": rope(64, 2), "t_rope_mla": rope(32, 4)}
    return {k: np.ascontiguousarray(v, dtype=np.float32) for k, v in f.items()}


_INS = ["x_prompt", "x_sample", "cache_mla_ckv", "cache_mla_krope", "cache_gqa_k", "cache_gqa_v", "c", "c_ctx",
        "w_ada", "b_ada", "g_norm1", "g_norm2", "w_in", "g_q_a", "w_q_up", "g_kv_a", "w_kv_up", "g_q_head",
        "g_k_head", "w_out", "w_ffn_gate", "w_ffn_up", "w_ffn_down", "g_final"]
_OUTS = [("y_prompt", (1, CTX, D_MODEL)), ("y_sample", (1, LAT, D_MODEL)), ("new_mla_ckv", (1, DEPTH, CTX, KVR)),
         ("new_mla_krope", (1, DEPTH, CTX, ROPE)), ("new_gqa_k", (1, DEPTH, CTX, 2, 64)),
         ("new_gqa_v", (1, DEPTH, CTX, 2, 64))]


def kernel(**inputs):
    import concourse.bacc as bacc
    from concourse.bass_utils import run_bass_kernel_spmd

    nc = bacc.Bacc("TRN2", target_bir_lowering=False, num_devices=1)
    arrays, a, o = {}, {}, {}
    for name, value in [(n, inputs[n]) for n in _INS] + list(tables().items()):
        value = np.ascontiguousarray(value)
        arrays[f"in_{name}"] = value
        a[name] = nc.dram_tensor(f"in_{name}", value.shape, mybir.dt.from_np(value.dtype), kind="ExternalInput").ap()
    for name, shape in _OUTS:
        o[name] = nc.dram_tensor(f"out_{name}", shape, F32, kind="ExternalOutput").ap()
    build(nc, a, o)
    r = run_bass_kernel_spmd(nc, [arrays], core_ids=[0])
    return tuple(r.results[0][f"out_{name}"] for name, _ in _OUTS)
```

```python
from contextlib import ExitStack

import numpy as np

import concourse.bass as bass
from concourse import mybir

F32 = mybir.dt.float32
F32R = mybir.dt.float32r
ALU = mybir.AluOpType
ACT = mybir.ActivationFunctionType
AX_X = mybir.AxisListType.X

P = 128
D_MODEL, DEPTH, EPS = 1024, 2, 1e-6
CTX, LAT, PAST = 128, 1024, 128
T = CTX + LAT
KEYS = CTX + PAST + LAT
KT = KEYS // P
DK = D_MODEL // P
G, GW = 3, T // 3
NOPE, ROPE, VD, HEADS = 64, 32, 64, 6
QR, KVR = 384, 256
D_FF = 2816
CHUNKS = D_FF // (2 * P)
MLA_SCALE = (NOPE + ROPE) ** -0.5
GQA_SCALE = VD ** -0.5
GRID_W = 64

PRE_LOADS = 22
DVE_STEPS = 51

IN_TILES = [("u", 672, 128), ("u", 800, 128), ("cq", 0, 128), ("cq", 128, 128), ("cq", 256, 128),
            ("ckv", 384, 128), ("ckv", 512, 128), ("kr", 640, 32), ("gk", 1312, 128), ("gv", 1440, 128),
            ("gq", 928, 128), ("gq", 1056, 128), ("gq", 1184, 128)]
N_IN, N_DFT, N_QUP, N_KVUP, N_OUT, N_FFN = len(IN_TILES), 2 * (LAT // P), 3, 2, DK, 6 * CHUNKS
U_DFT = N_IN
U_QUP = U_DFT + N_DFT
U_KVUP = U_QUP + N_QUP
U_OUT = U_KVUP + N_KVUP
U_FFN = U_OUT + N_OUT
UNITS = U_FFN + N_FFN
RING, STAGES = 6, 3


def loads_through(u):
    return sum(2 if U_QUP <= v < U_OUT else 1 for v in range(u % STAGES, u + 1, STAGES))


STAGE_LOADS = [loads_through(UNITS - STAGES + s) for s in range(STAGES)]
assert UNITS % RING == 0 and U_FFN % RING == 0 and RING % STAGES == 0

ROW = {"u": 0, "cq": 256, "ckv": 640, "gk": 896, "gq": 1024}
SCR_ROWS = 1408

E_DFT = G * N_IN
E_QUP = E_DFT + 9
E_V = E_QUP + 5 * G
E_K = E_V + KT
KGW, KG = KEYS // 4, 4
EVJ = E_K + 3 * KG
EV_SLOTS = 6

R_JOBS = ([("cq", 0, g) for g in range(G)] + [("gk", 0, g) for g in range(G)]
          + [("gq", m, g) for m in range(3) for g in range(G)] + [("ckv", 0, g) for g in range(G)]
          + [("rope", t, g) for t in range(2) for g in range(G)])


def sq_slot(r):
    return 0 if R_JOBS[r][0] in ("cq", "ckv") else r % 4


R_DFT = 15
R_NORMED = 18
STATS = 2 * G + R_NORMED
RO_SLOTS = 3
R_USES = []
for _r, (_kind, _t, _g) in enumerate(R_JOBS):
    for _i in range({"cq": 3, "ckv": 2}.get(_kind, 1)):
        _n = {"cq": 1, "gq": 1, "gk": 2 if _g == 0 else 1, "ckv": 1 if _g == 0 else 0}.get(_kind)
        if _kind == "rope":
            _n = 1 if _t == 0 else (3 if _g == 0 else 2)
        R_USES.append((_r, _i, _n))
assert len(R_USES) % RO_SLOTS == 0


def ev_stores(e):
    name = IN_TILES[e // G][0] if e < E_DFT else ""
    return 3 if name == "gv" and e % G == 0 else 1


def store_counts(stores, slots):
    total, after = [0] * slots, []
    for n, k in enumerate(stores):
        total[n % slots] += 16 * k
        after.append(total[n % slots])
    return after, total


EV_AFTER, EV_TOTAL = store_counts([ev_stores(e) for e in range(EVJ)], EV_SLOTS)
RO_AFTER, RO_TOTAL = store_counts([k for _, _, k in R_USES], RO_SLOTS)


def r_loads(kind, t):
    return {"cq": 1, "ckv": 1, "gk": 6, "gq": 6}.get(kind) or (10 if t == 0 else 8)


def raw_slot(r):
    return r % 4 if r < R_DFT else r % 2


RL_TOTAL, RL_AFTER = [0] * 4, []
for _r, (_kind, _t, _) in enumerate(R_JOBS):
    RL_TOTAL[raw_slot(_r)] += 16 * r_loads(_kind, _t)
    RL_AFTER.append(RL_TOTAL[raw_slot(_r)])

TILES, GROUPS = 18, 10
LAST_OF_GROUP = [9 * h + e for h in range(2) for e in (1, 3, 5, 7, 8)]
PAIRS = HEADS
PREP_AT = (3, 5, 7)
T_CHUNKS = [(0, 3), (3, 4), (7, 2)]


V_ORDER = [0] + list(range(2, KT)) + [1]


def is_ctx(s):
    return s % 9 == 8


def chunk_no(s, c=0):
    if s < 0:
        return chunk_no(s + TILES, c) - PAIR_CHUNKS
    return 25 * (s // 9) + 3 * (s % 9) + c


def chunks_of(s):
    return [(0, 0, 1)] if is_ctx(s) else [(c, k0, n) for c, (k0, n) in enumerate(T_CHUNKS)]


def chunks_through(s):
    return chunk_no(s) + len(chunks_of(s))


PAIR_CHUNKS = 50


def products_at(s, first, last):
    if s - 4 in LAST_OF_GROUP:
        return LAST_OF_GROUP.index(s - 4)
    if not first and s + TILES - 4 in LAST_OF_GROUP:
        return LAST_OF_GROUP.index(s + TILES - 4) - GROUPS
    return None


def steps_of(last):
    return range(2, TILES + (4 if last else 2))


ADA_PRE, ADA_AT = 4, (10, 19)
ADA_FIRST = 4 * ADA_PRE
ADA_LATE = 12 - ADA_PRE
assert ADA_LATE == 4 * len(ADA_AT)


def group_of(s):
    return 5 * (s // 9) + (s % 9) // 2


def build(nc, a, o):
    ctx = ExitStack()
    with ctx:
        FIRST_BYTE = -(-nc.sbuf_base // 64) * 64
        total = nc.sbuf_bytes_remaining // 64 * 64
        arena = ctx.enter_context(nc.sbuf_tensor("arena", [P, (total - 64) // 4], F32))
        base = FIRST_BYTE
        room = total - 128
        at = [0]

        def place(name, shape, dt, offset):
            return nc.alloc_sbuf_tensor_at(name, shape, dt, offset=base + offset)

        def keep(name, shape, dt=F32):
            size = int(np.prod(shape[1:])) * 4
            size += -size % 32
            at[0] += size
            return place(name, shape, dt, at[0] - size)

        x = keep("x", [P, DK, T])
        w_hi = keep("w_hi", [P, RING, 1024], F32R)
        w_lo = keep("w_lo", [P, RING, 1024], F32R)
        w_in_st = keep("w_stage", [P, STAGES, 1024])
        ring_at = at[0] - (2 * RING + STAGES) * 4096
        ada_buf = place("ada_buf", [P, 2, DK, 512], F32, ring_at)
        ada_row = place("ada_row", [P, 512], F32, ring_at + (RING + 2) * 4096)
        o_sum = place("o_sum", [P, 2, 256], F32, ring_at + (RING + 3) * 4096)
        wk = keep("wk", [P, 4, GW])
        kst = place("kst", [P, KEYS], F32, at[0] - 4 * GW * 4)
        rs_at = at[0]
        rs = keep("rs", [P, 3, GW])
        nt = keep("nt", [P, 3, GW])
        probs = place("probs", [P, 2, T], F32, rs_at)
        act_lo = place("act_lo", [P, 2, T], F32R, rs_at)
        ident = keep("ident", [P, P])
        ones = keep("ones", [P, P])
        head_ones = keep("head_ones", [P, P])
        mod = keep("mod", [P, DEPTH * 48, 2])
        vecs = keep("vecs", [P, 80])
        lmod = keep("lmod", [P, 48, 2])
        b_ada_t = keep("b_ada_t", [P, 96])
        lvec = keep("lvec", [P, 32])
        gs = keep("gs", [P, 2, DK, 2])
        silu_c = keep("silu_c", [P, 2, DK])
        chan_hi = keep("chan_hi", [P, 256], F32R)
        chan_lo = keep("chan_lo", [P, 256], F32R)
        cseq_hi = keep("cseq_hi", [P, 2, P], F32R)
        cseq_lo = keep("cseq_lo", [P, 2, P], F32R)
        eps_t = keep("eps_t", [P, 8])
        neg_max = keep("neg_max", [P, TILES])
        exp_sum = keep("exp_sum", [P, TILES])
        exp_inv = keep("exp_inv", [P, TILES])
        ph = at[0]

        def phase(first, *tensors):
            got, off = [], ph + first
            for name, shape, dt in tensors:
                got.append(place(name, shape, dt, off))
                off += int(np.prod(shape[1:])) * 4
            assert off <= room, (tensors[-1][0], off - room)
            return got

        h_hi, h_lo, act_hi = phase(0, ("h_hi", [P, DK, T], F32R), ("h_lo", [P, DK, T], F32R),
                                   ("act_hi", [P, 2, T], F32R))
        ev_p, = phase(2 * DK * T * 4, ("ev_p", [P, EV_SLOTS, GW], F32))
        EVB = EV_SLOTS * GW * 4
        ev_q, u_raw, u_hi, u_lo, a_hi, a_lo, r_raw, r_out = phase(
            0, ("ev_q", [P, EV_SLOTS, GW], F32), ("u_raw", [P, 2, T], F32), ("u_hi", [P, 2, T], F32R),
            ("u_lo", [P, 2, T], F32R), ("a_hi", [P, 9, 512], F32R), ("a_lo", [P, 9, 512], F32R),
            ("r_raw", [P, 2, 4, GW], F32), ("r_out", [P, RO_SLOTS, GW], F32))
        cache_t = place("cache_t", [P, 2, P], F32, rs_at + 3 * GW * 4)
        cq_raw, cq_hi, cq_lo, ckv_hi, ckv_lo = phase(
            EVB, ("cq_raw", [P, 3, T], F32), ("cq_hi", [P, 3, T], F32R), ("cq_lo", [P, 3, T], F32R),
            ("ckv_hi", [P, 2, KEYS], F32R), ("ckv_lo", [P, 2, KEYS], F32R))
        cache_in, = phase(EVB, ("cache_in", [P, 416], F32))
        ctx_in, nat_out = phase(2 * DK * T * 4, ("ctx_in", [P, 4, P], F32), ("nat_out", [P, 416], F32))
        qst, vst, mq_hi, mq_lo, mk_hi, mk_lo, mv, gq2, gk2, gk_lo, gv2, pt_hi, pt_lo, o_both = phase(
            0, ("qst", [P, T], F32), ("vst", [P, KT, VD], F32), ("mq_hi", [P, T], F32R), ("mq_lo", [P, T], F32R),
            ("mk_hi", [P, KEYS], F32R), ("mk_lo", [P, KEYS], F32R), ("mv", [P, KT, P], F32R),
            ("gq2", [P, T], F32R), ("gk2", [P, KEYS], F32R), ("gk_lo", [P, KEYS], F32R), ("gv2", [P, KT, P], F32R),
            ("pt_hi", [P, 2, 9, 256], F32R), ("pt_lo", [P, 2, 9, 256], F32R),
            ("o_both", [P, 2, 256], F32))
        r_more, = phase(EVB + 3 * T * 4, ("r_more", [P, 2, 4, GW], F32))
        ADA_SLOTS = 4
        ada_w, vec_rows, ada_rows, tab_in, x_in, pre_row = phase(
            0, ("ada_w", [P, ADA_SLOTS, DK, 512], F32), ("vec_rows", [80, P], F32), ("ada_rows", [96, P], F32),
            ("tab_in", [P, 512], F32), ("x_in", [P, 2, D_MODEL], F32),
            ("pre_row", [P, 2, 512], F32))
        y_out, = phase(0, ("y_out", [P, 2, D_MODEL], F32))

        ps = ctx.enter_context(nc.psum_tensor("ps", [P, 8, 512], F32))

        def dram(name, shape):
            return nc.dram_tensor(name, shape, F32, kind="Internal").ap()

        s_in = dram("s_in", (SCR_ROWS, T))
        s_cq = dram("s_cq", (QR, T))
        s_qn = dram("s_qn", (HEADS, NOPE, T))
        s_qr = dram("s_qr", (7 * ROPE, T))
        s_qrr = dram("s_qrr", (HEADS, ROPE, T))
        s_kn = dram("s_kn", (HEADS, NOPE, KEYS))
        s_kr = dram("s_kr", (ROPE, KEYS))
        s_gq = dram("s_gq", (HEADS, VD, T))
        s_gk = dram("s_gk", (2, VD, KEYS))
        s_v = dram("s_v", (KEYS, 8, VD))
        s_cc = dram("s_cc", (KVR, CTX))
        s_mix = dram("s_mix", (16, 64, T))

        def sem(name):
            return ctx.enter_context(nc.semaphore(name))

        unit_loaded = [sem(f"unit_loaded{i}") for i in range(STAGES)]
        unit_hi = sem("unit_hi")
        unit_split = sem("unit_split")
        dft_hi, dft_used = sem("dft_hi"), sem("dft_used")
        ev_mm, ev_done = sem("ev_mm"), sem("ev_done")
        ev_stored = [sem(f"ev_stored{i}") for i in range(EV_SLOTS)]
        lay_ready, sq_used = sem("lay_ready"), sem("sq_used")
        sq_done, stat_mm, stat_y0 = sem("sq_done"), sem("stat_mm"), sem("stat_y0")
        newt_a, newt_b, stat_rs = sem("newt_a"), sem("newt_b"), sem("stat_rs")
        nx_mul, nx_mod, nx_hi, nx_done = sem("nx_mul"), sem("nx_mod"), sem("nx_hi"), sem("nx_done")
        u_loaded, u_split = sem("u_loaded"), sem("u_split")
        ch_mm, ch_hi, ch_lo = sem("ch_mm"), sem("ch_hi"), sem("ch_lo")
        r_loaded = [sem(f"r_loaded{i}") for i in range(4)]
        r_sq, r_dve, r_use = sem("r_sq"), sem("r_dve"), sem("r_use")
        r_stored = [sem(f"r_stored{i}") for i in range(RO_SLOTS)]
        dve_step = sem("dve_step")
        cq_loaded, cq_split, ckv_split = sem("cq_loaded"), sem("cq_split"), sem("ckv_split")
        cache_loaded, cache_stored, ctx_loaded, nat_stored = (
            sem("cache_loaded"), sem("cache_stored"), sem("ctx_loaded"), sem("nat_stored"))
        gv_copied = sem("gv_copied")
        tr_mm, tr_ev = sem("tr_mm"), sem("tr_ev")
        q_loaded, k_loaded, v_loaded = sem("q_loaded"), sem("k_loaded"), sem("v_loaded")
        prep_hi, prep_q, prep_k, prep_v = sem("prep_hi"), sem("prep_q"), sem("prep_k"), sem("prep_v")
        s_mm, max_done, exp_done, inv_done, p_done = (
            sem("s_mm"), sem("max_done"), sem("exp_done"), sem("inv_done"), sem("p_done"))
        t_mm, pt_hi_done, pt_lo_done = sem("t_mm"), sem("pt_hi_done"), sem("pt_lo_done")
        pv_mm, both_done, o_done = sem("pv_mm"), sem("both_done"), sem("o_done")
        o_stored = [sem(f"o_stored{i}") for i in range(2)]
        mix_loaded = [sem(f"mix_loaded{i}") for i in range(4)]
        mix_hi, mix_split = sem("mix_hi"), sem("mix_split")
        out_mm, out_add = sem("out_mm"), sem("out_add")
        gate_mm, up_mm, silu_done, act_f, act_h, act_done = (
            sem("gate_mm"), sem("up_mm"), sem("silu_done"), sem("act_f"), sem("act_h"), sem("act_done"))
        down_mm, down_add = sem("down_mm"), sem("down_add")
        pre_loaded, pre_const, pre_ident, pre_tr, pre_vec, pre_silu, pre_tab = (
            sem("pre_loaded"), sem("pre_const"), sem("pre_ident"), sem("pre_tr"), sem("pre_vec"), sem("pre_silu"),
            sem("pre_tab"))
        x_loaded = [sem(f"x_loaded{i}") for i in range(2)]
        x_tr, x_ev_act, x_ev_dve = sem("x_tr"), sem("x_ev_act"), sem("x_ev_dve")
        ada_loaded = [sem(f"ada_loaded{i}") for i in range(ADA_SLOTS)]
        late_loaded = [sem(f"late_loaded{i}") for i in range(2)]
        late_mm, late_row, late_tr, late_ev = (
            sem("late_mm"), sem("late_row"), sem("late_tr"), sem("late_ev"))
        ada_row_done, ada_tr = sem("ada_row_done"), sem("ada_tr")
        ada_mm, ada_ev = sem("ada_mm"), sem("ada_ev")
        y_mod, y_tr, y_ev_act, y_ev_dve = sem("y_mod"), sem("y_tr"), sem("y_ev_act"), sem("y_ev_dve")
        y_stored = [sem(f"y_stored{i}") for i in range(2)]

        w_in_v = a["w_in"].rearrange("l (k p) n -> l p k n", p=P)
        w_q_up_v = a["w_q_up"].rearrange("l (k p) (h n) -> l k p h n", p=P, h=HEADS)
        w_kv_up_v = a["w_kv_up"].rearrange("l (k p) (h c n) -> l k c p h n", p=P, h=HEADS, c=2)
        w_out_v = a["w_out"].rearrange("l (k p) n -> l p k n", p=P)
        w_gate_v = a["w_ffn_gate"].rearrange("l (k p) (c t n) -> l c t p k n", p=P, t=2, n=P)
        w_up_v = a["w_ffn_up"].rearrange("l (k p) (c t n) -> l c t p k n", p=P, t=2, n=P)
        w_down_v = a["w_ffn_down"].rearrange("l (c k p) (h n) -> l c h p k n", k=2, p=P, h=2)
        w_ada_v = a["w_ada"].rearrange("l (k p) (q n) -> l q p k n", p=P, n=512)
        mix_v = s_mix.rearrange("h r t -> (h r) t")

        def cols(g):
            return slice(g * GW, (g + 1) * GW)

        def key_pieces(g):
            if g == 0:
                return [(0, CTX, 0), (CTX, GW, CTX + PAST)]
            return [(0, GW, g * GW + PAST)]

        def halves(g):
            return [(0, 0, CTX), (1, CTX, GW)] if g == 0 else [(1, g * GW, (g + 1) * GW)]

        ps_flat = ps.rearrange("p b n -> p (b n)")

        def s_place(s):
            return ps_flat[:, 1536 * (s % 2):1536 * (s % 2) + T]

        def t_place(r, c):
            return [(3 * ((r + 1) % 2) + 2, P), (6, 0), (7, 256)][c]

        def raw_of(r):
            slot = raw_slot(r)
            return (r_raw if slot < 2 else r_more)[:, slot % 2]

        def unit_width(u):
            if u < U_DFT:
                return DK * IN_TILES[u][2]
            if U_QUP <= u < U_KVUP:
                return HEADS * (NOPE + ROPE)
            if U_KVUP <= u < U_OUT:
                return HEADS * (NOPE + VD)
            return 1024

        def wtiles(u, n):
            s = u % RING
            w = unit_width(u) if u < U_FFN else 1024
            return [t[:, s, 0:w].rearrange("p (k n) -> p k n", n=n) for t in (w_hi, w_lo)]

        block = ctx.enter_context(nc.Block())

        settled = {nc.sync: sem("settled_sp"), nc.gpsimd: sem("settled_pool"), nc.tensor: sem("settled_pe"),
                   nc.scalar: sem("settled_act")}

        def settle(eng):
            eng.sem_inc(settled[eng], 1)

        @block.sync
        def _(sp):
            for src, r0, rn in (("c_ctx", 0, 8), ("c", 8, 8)):
                v = a[src] if src == "c_ctx" else a[src].rearrange("a d -> (a d)")
                sp.dma_start(vec_rows[r0:r0 + rn, :], v.rearrange("(k p) -> k p", p=P)).then_inc(pre_loaded, 16)
            sp.dma_start(vec_rows[16:32, :], a["g_norm1"].rearrange("l (k p) -> (l k) p", p=P)).then_inc(pre_loaded, 16)
            sp.dma_start(vec_rows[32:48, :], a["g_norm2"].rearrange("l (k p) -> (l k) p", p=P)).then_inc(pre_loaded, 16)
            sp.dma_start(vec_rows[48:56, :], a["g_final"].rearrange("(k p) -> k p", p=P)).then_inc(pre_loaded, 16)
            sp.dma_start(vec_rows[56:62, :], a["g_q_a"].rearrange("l (k p) -> (l k) p", p=P)).then_inc(pre_loaded, 16)
            sp.dma_start(vec_rows[62:66, :], a["g_kv_a"].rearrange("l (k p) -> (l k) p", p=P)).then_inc(pre_loaded, 16)
            for j, name in enumerate(("g_q_head", "g_k_head")):
                r0 = 66 + 2 * j
                sp.dma_start(vec_rows[r0:r0 + 2, 0:64], a[name]).then_inc(pre_loaded, 16)
                sp.dma_start(vec_rows[r0:r0 + 2, 64:128], a[name]).then_inc(pre_loaded, 16)
                for q in range(4):
                    sp.dma_start(vec_rows[r0 + 4:r0 + 6, 32 * q:32 * q + 32],
                                 a[name][:, 32 * (1 - q % 2):32 * (1 - q % 2) + 32]).then_inc(pre_loaded, 16)
            sp.dma_start(ada_rows[:, :], a["b_ada"].rearrange("l (k p) -> (l k) p", p=P)).then_inc(pre_loaded, 16)
            sp.dma_start(tab_in[:, 0:256], a["t_chan"]).then_inc(pre_loaded, 16)
            sp.dma_start(tab_in[:, 256:512], a["t_ctx"]).then_inc(pre_loaded, 16)
            for i in range(9):
                if i >= 2:
                    sp.wait_ge(x_tr, 2 * (i - 1))
                src = a["x_prompt"][0] if i == 0 else a["x_sample"][0, (i - 1) * P:i * P, :]
                sp.dma_start(x_in[:, i % 2, :], src).then_inc(x_loaded[i % 2], 16)
            for i in range(DEPTH * ADA_PRE):
                s = i % ADA_SLOTS
                if i >= ADA_SLOTS:
                    sp.wait_ge(ada_mm, i - ADA_SLOTS + 1)
                sp.dma_start(ada_w[:, s, :, :], w_ada_v[i // ADA_PRE, i % ADA_PRE]).then_inc(ada_loaded[s], 16)

            with sp.Fori(0, DEPTH) as l:
                def load_unit(u, src, dst_shape=None, c0=0, c1=None):
                    s = u % STAGES
                    sp.wait_ge(unit_split, l * UNITS + u + 1)
                    settle(sp)
                    dst = w_in_st[:, s, c0:c1 or unit_width(u)]
                    if dst_shape:
                        dst = dst.rearrange("p (k n) -> p k n", n=dst_shape)
                    sp.dma_start(dst, src).then_inc(unit_loaded[s], 16)

                def wait_ev_stored(jobs):
                    need = {}
                    for e in jobs:
                        need[e % EV_SLOTS] = max(need.get(e % EV_SLOTS, 0), EV_AFTER[e])
                    for s, v in sorted(need.items()):
                        sp.wait_ge(ev_stored[s], l * EV_TOTAL[s] + v)
                        settle(sp)

                def wait_ro_stored(uses):
                    need = {}
                    for e in uses:
                        need[e % RO_SLOTS] = max(need.get(e % RO_SLOTS, 0), RO_AFTER[e])
                    for s, v in sorted(need.items()):
                        sp.wait_ge(r_stored[s], l * RO_TOTAL[s] + v)
                        settle(sp)

                def load_r(r):
                    kind, t, g = R_JOBS[r]
                    s = raw_slot(r)
                    if 4 <= r < R_DFT:
                        sp.wait_ge(r_dve, l * len(R_JOBS) + r - 3)
                        settle(sp)
                    elif r >= R_DFT:
                        sp.wait_ge(r_dve, l * len(R_JOBS) + r - 1)
                        settle(sp)

                    raw = raw_of(r)

                    def get(dst, src):
                        sp.dma_start(dst, src).then_inc(r_loaded[s], 16)

                    if kind in ("cq", "ckv"):
                        if g == 0:
                            first = [x_[0] for x_ in IN_TILES].index(kind)
                            wait_ev_stored(range(G * first, G * (first + (3 if kind == "cq" else 2))))
                        k = 3 if kind == "cq" else 2
                        rows = s_in[ROW[kind]:ROW[kind] + k * P, cols(g)]
                        get(raw[:, 0:k, :], rows.rearrange("(k p) t -> p k t", p=P))
                    elif kind in ("gk", "gq"):
                        u = [x_[0] for x_ in IN_TILES].index(kind) + t
                        wait_ev_stored([G * u + g])
                        r0 = ROW[kind] + t * P
                        get(raw[:, 0, :], s_in[r0:r0 + P, cols(g)])
                        for q in range(4):
                            q2 = q ^ 1
                            get(raw[32 * q:32 * q + 32, 1, :], s_in[r0 + 32 * q2:r0 + 32 * q2 + 32, cols(g)])
                        get(raw[:, 2:4, :], a["t_rope_gqa"][:, :, cols(g)])
                    else:
                        wait_ev_stored([E_QUP + 5 * g + 3 + t] + ([G * 7 + g] if t else []))
                        r0, n = (0, 8) if t == 0 else (P, 6)
                        get(raw[0:16 * n, 0, :], s_qr[r0:r0 + 16 * n, cols(g)])
                        for q in range(n):
                            q2 = q ^ 1
                            get(raw[16 * q:16 * q + 16, 1, :], s_qr[r0 + 16 * q2:r0 + 16 * q2 + 16, cols(g)])
                        get(raw[:, 2:4, :], a["t_rope_mla"][:, :, cols(g)])

                for u, (_, c0, w) in enumerate(IN_TILES):
                    load_unit(u, w_in_v[l, :, :, c0:c0 + w], w)
                sp.dma_start(s_v[CTX:CTX + PAST, HEADS:8, :], a["cache_gqa_v"][0, l]).then_inc(gv_copied, 16)

                def load_dft(i):
                    load_unit(U_DFT + i, a["t_seq"][i // 2, :, i % 2, :])

                for i in range(RING):
                    load_dft(i)
                wait_ev_stored(range(0, 2 * G))
                sp.wait_ge(ev_mm, l * EVJ + E_DFT)
                sp.dma_start(u_raw[:, :, :], s_in[0:256, :].rearrange("(k p) t -> p k t", p=P)).then_inc(u_loaded, 16)
                wait_ev_stored(range(E_DFT - EV_SLOTS, E_DFT))
                load_r(0)
                load_r(1)
                sp.wait_ge(ch_mm, l * 9 + 9)
                settle(sp)
                load_r(2)
                load_r(3)
                for i in range(RING, N_DFT):
                    load_dft(i)
                    load_r(i - RING + 4)
                for r in range(N_DFT - RING + 4, R_DFT):
                    load_r(r)
                for k in range(N_QUP):
                    load_unit(U_QUP + k, w_q_up_v[l, k, :, :, 0:NOPE], NOPE, 0, HEADS * NOPE)
                    sp.dma_start(w_in_st[:, (U_QUP + k) % STAGES, HEADS * NOPE:HEADS * (NOPE + ROPE)]
                                 .rearrange("p (h n) -> p h n", n=ROPE), w_q_up_v[l, k, :, :, NOPE:])\
                        .then_inc(unit_loaded[(U_QUP + k) % STAGES], 16)
                wait_ro_stored([n for n, (r, _, _) in enumerate(R_USES) if R_JOBS[r][0] == "cq"])
                sp.dma_start(cq_raw[:, :, :], s_cq.rearrange("(k p) t -> p k t", p=P)).then_inc(cq_loaded, 16)
                for k in range(N_KVUP):
                    load_unit(U_KVUP + k, w_kv_up_v[l, k, 0], NOPE, 0, HEADS * NOPE)
                    sp.dma_start(w_in_st[:, (U_KVUP + k) % STAGES, HEADS * NOPE:HEADS * (NOPE + VD)]
                                 .rearrange("p (h n) -> p h n", n=VD), w_kv_up_v[l, k, 1])\
                        .then_inc(unit_loaded[(U_KVUP + k) % STAGES], 16)
                for r in range(R_DFT, R_NORMED):
                    load_r(r)
                sp.wait_ge(cq_split, l * G + G)
                sp.dma_start(cache_in[:, 0:256], a["cache_mla_ckv"][0, l]).then_inc(cache_loaded, 16)
                sp.dma_start(cache_in[:, 256:288], a["cache_mla_krope"][0, l]).then_inc(cache_loaded, 16)
                sp.dma_start(cache_in[:, 288:416], a["cache_gqa_k"][0, l].rearrange("t h d -> t (h d)"))\
                    .then_inc(cache_loaded, 16)
                for r in range(R_NORMED, len(R_JOBS)):
                    load_r(r)
                for m in range(STAGES):
                    load_unit(U_OUT + m, w_out_v[l, :, :, m * P:(m + 1) * P], P)
                sp.wait_ge(tr_ev, l * 5 + 4)
                sp.dma_start(s_gk[:, :, CTX:CTX + PAST].rearrange("h r t -> (h r) t"), cache_t[:, 1, :])\
                    .then_inc(cache_stored, 16)
                sp.dma_start(s_kr[:, CTX:CTX + PAST], cache_t[0:ROPE, 0, :]).then_inc(cache_stored, 16)
                wait_ro_stored(range(len(R_USES)))
                wait_ev_stored(range(EVJ - EV_SLOTS, EVJ))
                sp.wait_ge(cache_stored, (l + 1) * 32)
                settle(sp)
                sp.wait_ge(gv_copied, (l + 1) * 16)
                settle(sp)

                def load_mla(p, y):
                    sp.wait_ge(prep_q, y)
                    sp.dma_start(qst[0:NOPE, :], s_qn[p]).then_inc(q_loaded, 16)
                    sp.dma_start(qst[NOPE:96, :], s_qrr[p]).then_inc(q_loaded, 16)
                    sp.wait_ge(prep_k, y)
                    sp.dma_start(kst[0:NOPE, :], s_kn[p]).then_inc(k_loaded, 16)
                    sp.dma_start(kst[NOPE:96, :], s_kr).then_inc(k_loaded, 16)
                    sp.wait_ge(prep_v, y)
                    sp.dma_start(vst[:, :, :], s_v.rearrange("(k q) h d -> h q k d", q=P)[p]).then_inc(v_loaded, 16)

                def load_gqa(p, kv, y):
                    sp.wait_ge(prep_q, y)
                    for half in range(2):
                        sp.dma_start(qst[64 * half:64 * half + 64, :], s_gq[p]).then_inc(q_loaded, 16)
                    sp.wait_ge(prep_k, y)
                    for half in range(2):
                        sp.dma_start(kst[64 * half:64 * half + 64, :], s_gk[kv]).then_inc(k_loaded, 16)
                    sp.wait_ge(prep_v, y)
                    sp.dma_start(vst[:, :, :], s_v.rearrange("(k q) h d -> h q k d", q=P)[HEADS + kv])\
                        .then_inc(v_loaded, 16)

                def store_o(p, pi, g):
                    sp.wait_ge(o_done, pi * GROUPS + g + 1)
                    settle(sp)
                    row = p if g < 5 else 10 + p
                    c0, n = (0, CTX) if g % 5 == 4 else (CTX + 256 * (g % 5), 256)
                    sp.dma_start(s_mix[row, :, c0:c0 + n], o_sum[0:64, g % 2, 0:n]).then_inc(o_stored[g % 2], 16)

                load_mla(0, l * 12)

                def load_ada(p, j):
                    if j == 0:
                        sp.wait_ge(late_mm, l * ADA_LATE + (p - 1) * 2)
                        settle(sp)
                    w, k = j // 4, 2 * (j % 4)
                    sp.dma_start(ada_buf[:, w, k:k + 2, :], w_ada_v[l, ADA_PRE + (p - 1) * 2 + w][:, k:k + 2, :])\
                        .then_inc(late_loaded[w], 16)

                def pair(p, kv, first=False, last=False):
                    pi = l * PAIRS + p
                    load_gqa(p, kv, pi * 2 + 1)
                    for n in range(GROUPS):
                        g = n - 2
                        if g == 3 and not last:
                            load_mla(p + 1, pi * 2 + 2)
                        if g >= 0:
                            store_o(p, pi, g)
                        elif not first:
                            store_o(p - 1, pi - 1, GROUPS + g)
                        if not first and not last and n < 8:
                            load_ada(p, n)
                    if last:
                        for g in range(GROUPS - 2, GROUPS):
                            store_o(p, pi, g)

                pair(0, 0, first=True)
                with sp.Fori(1, 3) as p:
                    pair(p, 0)
                with sp.Fori(3, 5) as p:
                    pair(p, 1)
                pair(5, 1, last=True)

                for i in range(2):
                    sp.wait_ge(o_stored[i], (l + 1) * (PAIRS * GROUPS // 2 * 16))
                for i in range(G * DK):
                    g, k = divmod(i, DK)
                    if i >= 4:
                        sp.wait_ge(mix_split, l * G * DK + i - 3)
                    sp.dma_start(wk[:, i % 4, :], mix_v[k * P:(k + 1) * P, cols(g)]).then_inc(mix_loaded[i % 4], 16)
                sp.dma_start(ctx_in[:, 0:2, :], s_cc.rearrange("(k p) t -> p k t", p=P)).then_inc(ctx_loaded, 16)
                sp.dma_start(ctx_in[0:ROPE, 2, :], s_kr[:, 0:CTX]).then_inc(ctx_loaded, 16)
                sp.dma_start(ctx_in[:, 3, :], s_gk[:, :, 0:CTX].rearrange("h r t -> (h r) t"))\
                    .then_inc(ctx_loaded, 16)
                for m in range(STAGES, N_OUT):
                    load_unit(U_OUT + m, w_out_v[l, :, :, m * P:(m + 1) * P], P)
                sp.wait_ge(tr_ev, (l + 1) * 5)
                settle(sp)
                sp.dma_start(o["new_mla_ckv"][0, l], nat_out[:, 0:256]).then_inc(nat_stored, 16)
                sp.dma_start(o["new_mla_krope"][0, l], nat_out[:, 256:288]).then_inc(nat_stored, 16)
                sp.dma_start(o["new_gqa_k"][0, l].rearrange("t h d -> t (h d)"), nat_out[:, 288:416])\
                    .then_inc(nat_stored, 16)
                with sp.Fori(0, CHUNKS) as c:
                    for j in range(6):
                        s = (U_FFN + j) % STAGES
                        sp.wait_ge(unit_split, l * UNITS + c * 6 + U_FFN + j + 1)
                        if j < 4:
                            src = (w_gate_v, w_up_v)[j % 2][l, c, j // 2]
                            dst = w_in_st[:, s, :].rearrange("p (k n) -> p k n", n=P)
                        else:
                            src = w_down_v[l, c, j - 4]
                            dst = w_in_st[:, s, :].rearrange("p (k n) -> p k n", n=512)
                        sp.dma_start(dst, src).then_inc(unit_loaded[s], 16)

            for i in range(9):
                sp.wait_ge(y_ev_act, i + 1)
                sp.wait_ge(y_ev_dve, i + 1)
                dst = o["y_prompt"][0] if i == 0 else o["y_sample"][0, (i - 1) * P:i * P, :]
                sp.dma_start(dst, y_out[:, i % 2, :]).then_inc(y_stored[i % 2], 16)
            sp.wait_ge(y_stored[0], 5 * 16)
            sp.wait_ge(y_stored[1], 4 * 16)
            for s in range(EV_SLOTS):
                sp.wait_ge(ev_stored[s], DEPTH * EV_TOTAL[s])
            sp.wait_ge(nat_stored, DEPTH * 48)

        @block.gpsimd
        def _(pool):
            pool.memset(ident[:, :], 0.0).then_inc(pre_ident, 1)
            pool.wait_ge(pre_ident, 1)
            pool.affine_select(out=ident[:, :], in_=ident[:, :], compare_op=ALU.not_equal, fill=1.0, base=0,
                               pattern=[[-1, P]], channel_multiplier=1).then_inc(pre_ident, 1)

            with pool.Fori(0, DEPTH) as l:
                def wait_slot_used(u):
                    if u < 0:
                        pool.wait_ge(down_mm, l * (CHUNKS * G * DK))
                    elif u < U_DFT:
                        pool.wait_ge(ev_mm, l * EVJ + G * (u + 1))
                    elif u < U_QUP - 1:
                        pool.wait_ge(dft_used, l * (N_DFT - 1) + u - U_DFT + 1)
                    elif u < U_OUT:
                        pool.wait_ge(ev_mm, l * EVJ + (E_QUP if u < U_QUP else E_V if u < U_KVUP else EVJ))
                    else:
                        pool.wait_ge(out_mm, l * G * DK + G * (u - U_OUT + 1))

                def split_unit(u):
                    s, st, w = u % RING, u % STAGES, unit_width(u)
                    pool.wait_ge(unit_loaded[st], l * (STAGE_LOADS[st] * 16) + loads_through(u) * 16)
                    wait_slot_used(u - RING)
                    if U_DFT <= u < U_QUP:
                        pool.wait_ge(dft_hi, l * N_DFT + u - U_DFT + 1)
                    else:
                        n = l * (UNITS - N_DFT) + (u if u < U_DFT else u - N_DFT)
                        settle(pool)
                        pool.tensor_copy(w_hi[:, s, 0:w], w_in_st[:, st, 0:w]).then_inc(unit_hi, 1)
                        pool.wait_ge(unit_hi, n + 1)
                    pool.tensor_tensor(w_lo[:, s, 0:w], w_in_st[:, st, 0:w], w_hi[:, s, 0:w].bitcast(F32),
                                       ALU.subtract).then_inc(unit_split, 1)

                def norm_mul(n0, stat0):
                    pool.wait_ge(sq_used, n0 + G * DK + 4)
                    for i in range(G * DK):
                        g, k = divmod(i, DK)
                        if k == 0:
                            pool.wait_ge(stat_rs, stat0 + g + 1)
                        if i >= 4:
                            pool.wait_ge(nx_done, n0 + i - 3)
                        pool.tensor_tensor(wk[:, i % 4, :], x[:, k, cols(g)], rs[:, g, :], ALU.mult)\
                            .then_inc(nx_mul, 1)

                for u in range(4):
                    split_unit(u)
                norm_mul(l * (2 * G * DK), l * STATS)
                for u in range(4, U_OUT):
                    split_unit(u)

                def low_steps(mla, y):
                    def q_low(tiles_done=0):
                        pool.wait_ge(prep_hi, y * 3 + 1)
                        if mla:
                            ins = pool.tensor_tensor(mq_lo[0:96, :], qst[0:96, :], mq_hi[0:96, :].bitcast(F32),
                                                     ALU.subtract)
                        else:
                            pool.wait_ge(p_done, tiles_done)
                            ins = pool.tensor_tensor(gq2[64:P, :], qst[64:P, :], gq2[64:P, :].bitcast(F32),
                                                     ALU.subtract)
                        ins.then_inc(prep_q, 1)
                        pool.wait_ge(prep_q, y + 1)

                    def k_low(tiles_done=0):
                        pool.wait_ge(prep_hi, y * 3 + 2)
                        lo, n, hi = (mk_lo, 96, mk_hi) if mla else (gk_lo, 64, gk2)
                        pool.tensor_tensor(lo[0:n, :], kst[0:n, :], hi[0:n, :].bitcast(F32), ALU.subtract)\
                            .then_inc(prep_k, 1)

                    def v_low(tiles_done=0):
                        pool.wait_ge(prep_hi, y * 3 + 3)
                        v2 = mv if mla else gv2
                        pool.tensor_tensor(v2[:, :, VD:P], vst[:, :, :], v2[:, :, 0:VD].bitcast(F32), ALU.subtract)\
                            .then_inc(prep_v, 1)

                    return q_low, k_low, v_low

                for step in low_steps(True, l * 12):
                    step()

                def pair(p, last=False):
                    pi = l * PAIRS + p
                    steps = [low_steps(False, pi * 2 + 1), () if last else low_steps(True, pi * 2 + 2)]
                    for s in range(TILES):
                        pool.wait_ge(inv_done, pi * TILES + s + 1)
                        settle(pool)
                        n = P if is_ctx(s) else T
                        pool.tensor_scalar(probs[:, s % 2, 0:n], probs[:, s % 2, 0:n], exp_inv[:, s:s + 1], 1.0,
                                           ALU.mult, ALU.mult).then_inc(p_done, 1)
                        if s % 9 in PREP_AT and steps[s // 9]:
                            steps[s // 9][PREP_AT.index(s % 9)](pi * TILES + s + 1)
                        elif last and s % 9 in PREP_AT:
                            if s % 9 == PREP_AT[0]:
                                pool.wait_ge(late_ev, (l + 1) * ADA_LATE)
                                settle(pool)
                            split_unit(U_OUT + PREP_AT.index(s % 9))

                with pool.Fori(0, 3) as p:
                    pair(p)
                with pool.Fori(3, 5) as p:
                    pair(p)
                pair(5, last=True)

                for i in range(2):
                    pool.wait_ge(o_stored[i], (l + 1) * (PAIRS * GROUPS // 2 * 16))
                settle(pool)
                for u in range(U_OUT + STAGES, U_FFN + 4):
                    split_unit(u)
                norm_mul(l * (2 * G * DK) + G * DK, l * STATS + STATS - G)
                for u in range(U_FFN + 4, U_FFN + 6):
                    split_unit(u)
                with pool.Fori(1, CHUNKS) as c:
                    for j in range(6):
                        s, st = j, j % STAGES
                        n = l * UNITS + c * 6 + U_FFN + j
                        pool.wait_ge(unit_loaded[st], l * (STAGE_LOADS[st] * 16) + c * (6 // STAGES * 16)
                                     + loads_through(U_FFN + j) * 16)
                        if j < 4:
                            pool.wait_ge((gate_mm, up_mm)[j % 2], l * (CHUNKS * 6) + c * 6 - 6 + 3 * (j // 2 + 1))
                        else:
                            pool.wait_ge(down_mm, l * (CHUNKS * G * DK) + c * (G * DK) - 8 + 4 * (j - 3))
                        settle(pool)
                        pool.tensor_copy(w_hi[:, s, :], w_in_st[:, st, :]).then_inc(unit_hi, 1)
                        pool.wait_ge(unit_hi, l * (UNITS - N_DFT) + c * 6 + U_FFN - N_DFT + j + 1)
                        pool.tensor_tensor(w_lo[:, s, :], w_in_st[:, st, :], w_hi[:, s, :].bitcast(F32),
                                           ALU.subtract).then_inc(unit_split, 1)

            for i in range(G * DK):
                g, k = divmod(i, DK)
                pool.wait_ge(sq_used, (2 * DEPTH + 1) * G * DK + 4)
                pool.wait_ge(stat_rs, DEPTH * STATS + g + 1)
                if i >= 4:
                    pool.wait_ge(y_mod, i - 3)
                pool.tensor_tensor(wk[:, i % 4, :], x[:, k, cols(g)], rs[:, g, :], ALU.mult).then_inc(nx_mul, 1)

        @block.scalar
        def _(act):
            act.wait_ge(pre_vec, 2)
            nc.scalar.activation(silu_c[:, :, :], vecs[:, 0:16].rearrange("p (c k) -> p c k", c=2), ACT.Silu)\
                .then_inc(pre_silu, 1)
            for i in range(9):
                act.wait_ge(x_tr, 2 * i + 1)
                nc.scalar.activation(x[:, 0:4, i * P:(i + 1) * P], ps[:, 0, :].rearrange("p (k t) -> p k t", k=4),
                                     ACT.Copy).then_inc(x_ev_act, 1)

            def root(stat, bank, dim):
                act.wait_ge(stat_rs, stat)
                nc.scalar.activation(nt[:, 0, :], ps[:, bank, 0:GW], ACT.Copy, bias=EPS, scale=1.0 / dim)
                nc.scalar.activation(nt[:, 1, :], ps[:, bank, 0:GW], ACT.Abs_reciprocal_sqrt, bias=eps_t[:, 0:1],
                                     scale=1.0 / dim).then_inc(stat_y0, 1)

            def norm_x(stat0, n0, which, out0=0):
                if which == 1:
                    act.wait_ge(mix_split, out0 + G * DK)
                for i in range(G * DK):
                    if which == 1:
                        k, g = divmod(i, G)
                        act.wait_ge(out_add, out0 + i + 1)
                    else:
                        g, k = divmod(i, DK)
                    act.wait_ge(sq_used, n0 + i + 1)
                    nc.scalar.activation(wk[:, i % 4, :], x[:, k, cols(g)], ACT.Square).then_inc(sq_done, 1)
                for g in range(G):
                    act.wait_ge(sq_used, n0 + 4 + (G * DK - G + g + 1 if which == 1 else (g + 1) * DK))
                    root(stat0 + g, 5 + g, D_MODEL)
                if which is None:
                    return
                for i in range(G * DK):
                    g, k = divmod(i, DK)
                    act.wait_ge(nx_mul, n0 + i + 1)
                    for c, c0, c1 in halves(g):
                        v = wk[:, i % 4, c0 - g * GW:c1 - g * GW]
                        ins = nc.scalar.activation(v, v, ACT.Identity, bias=lmod[:, 24 * which + k, c:c + 1],
                                                   scale=gs[:, which, k, c:c + 1])
                    ins.then_inc(nx_mod, 1)

            with act.Fori(0, DEPTH) as l:
                act.wait_ge(lay_ready, l + 1)
                norm_x(l * STATS, l * (2 * G * DK), 0)

                def store_ev(e, ev):
                    act.wait_ge(ev_done, l * EVJ + e + 1)
                    s = e % EV_SLOTS

                    def put(dst, src):
                        act.dma_start(dst, src).then_inc(ev_stored[s], 16)

                    if e < E_DFT:
                        u, g = divmod(e, G)
                        name, _, w = IN_TILES[u]
                        t = u - [x_[0] for x_ in IN_TILES].index(name)
                        if name == "kr":
                            put(s_qr[6 * ROPE:7 * ROPE, cols(g)], ev[0:ROPE, s, :])
                        elif name == "gv":
                            flat = s_v.rearrange("t h d -> t (h d)")[:, HEADS * VD:8 * VD]
                            if g == 0:
                                put(flat[0:CTX, :], ev[:, s, 0:P])
                                put(o["new_gqa_v"][0, l].rearrange("t h d -> t (h d)"), ev[:, s, 0:P])
                                put(flat[2 * P:4 * P, :].rearrange("(k q) d -> q k d", q=P),
                                    ev[:, s, P:3 * P].rearrange("q (k d) -> q k d", d=P))
                            else:
                                k0 = (3 * g + 1) * P
                                put(flat[k0:k0 + GW, :].rearrange("(k q) d -> q k d", q=P),
                                    ev[:, s, :].rearrange("q (k d) -> q k d", d=P))
                        else:
                            r0 = ROW[name] + t * P
                            put(s_in[r0:r0 + P, cols(g)], ev[:, s, :])
                    elif e == E_DFT:
                        put(mix_v[384:640, 0:CTX].rearrange("(f q) t -> q f t", q=P),
                            ev[:, s, 0:256].rearrange("q (f t) -> q f t", f=2))
                    elif e < E_QUP:
                        j = e - E_DFT - 1
                        r0, c0 = 384 + P * (j // 4), CTX + 256 * (j % 4)
                        put(mix_v[r0:r0 + P, c0:c0 + 256], ev[:, s, 0:256])
                    elif e < E_V:
                        g, mt = divmod(e - E_QUP, 5)
                        if mt < 3:
                            put(s_qn.rearrange("h r t -> (h r) t")[mt * P:(mt + 1) * P, cols(g)], ev[:, s, :])
                        else:
                            n = P if mt == 3 else 64
                            put(s_qr[(mt - 3) * P:(mt - 3) * P + n, cols(g)], ev[0:n, s, :])
                    elif e < E_K:
                        i = V_ORDER[e - E_V]
                        put(s_v.rearrange("t h d -> t (h d)")[i * P:(i + 1) * P, 0:HEADS * VD], ev[:, s, :])
                    else:
                        mt, kg = divmod(e - E_K, KG)
                        put(s_kn.rearrange("h r t -> (h r) t")[mt * P:(mt + 1) * P, kg * KGW:(kg + 1) * KGW],
                            ev[:, s, 0:KGW])

                def evacuate(e, ev, bank, rows, n, col=0, scale=1.0):
                    s = e % EV_SLOTS
                    act.wait_ge(ev_mm, l * EVJ + e + 1)
                    before = l * EV_TOTAL[s] + (EV_AFTER[e - EV_SLOTS] if e >= EV_SLOTS else 0)
                    act.wait_ge(ev_stored[s], before)
                    nc.scalar.activation(ev[0:rows, s, 0:n], ps[0:rows, bank, col:col + n], ACT.Copy, scale=scale)\
                        .then_inc(ev_done, 1)

                for e in range(E_DFT):
                    evacuate(e, ev_p, e % 6, IN_TILES[e // G][2], GW)
                    if e:
                        store_ev(e - 1, ev_p)
                store_ev(E_DFT - 1, ev_p)

                def r_squares(r):
                    kind, t, g = R_JOBS[r]
                    k = {"cq": 3, "ckv": 2}.get(kind, 1)
                    act.wait_ge(r_loaded[raw_slot(r)], l * RL_TOTAL[raw_slot(r)] + RL_AFTER[r])
                    act.wait_ge(stat_mm, l * R_NORMED + (r - 1 if r >= 4 and k == 1 else r))
                    nc.scalar.activation(wk[:, sq_slot(r):sq_slot(r) + k, :], raw_of(r)[:, 0:k, :], ACT.Square)\
                        .then_inc(r_sq, 1)

                def r_root(r):
                    kind = R_JOBS[r][0]
                    act.wait_ge(stat_mm, l * R_NORMED + r + 1)
                    root(l * STATS + G + r, 4 + r % 2, {"cq": QR, "ckv": KVR}.get(kind, 64))

                def r_store(r):
                    kind, t, g = R_JOBS[r]
                    for n, (r_, i, k) in enumerate(R_USES):
                        if r_ != r or not k:
                            continue
                        s = n % RO_SLOTS
                        act.wait_ge(r_use, l * len(R_USES) + n + 1)

                        def put(dst, src):
                            act.dma_start(dst, src).then_inc(r_stored[s], 16)

                        if kind == "cq":
                            put(s_cq[i * P:(i + 1) * P, cols(g)], r_out[:, s, :])
                        elif kind == "gq":
                            put(s_gq.rearrange("h r t -> (h r) t")[t * P:(t + 1) * P, cols(g)], r_out[:, s, :])
                        elif kind == "gk":
                            for c0, c1, k0 in key_pieces(g):
                                put(s_gk.rearrange("h r t -> (h r) t")[:, k0:k0 + c1 - c0], r_out[:, s, c0:c1])
                        elif kind == "ckv":
                            put(s_cc[i * P:(i + 1) * P, :], r_out[:, s, 0:CTX])
                        elif t == 0:
                            put(s_qrr.rearrange("h r t -> (h r) t")[0:P, cols(g)], r_out[:, s, :])
                        else:
                            put(s_qrr.rearrange("h r t -> (h r) t")[P:6 * ROPE, cols(g)], r_out[0:64, s, :])
                            for c0, c1, k0 in key_pieces(g):
                                put(s_kr[:, k0:k0 + c1 - c0], r_out[64:96, s, c0:c1])

                for i in range(9):
                    act.wait_ge(ch_mm, l * 9 + i + 1)
                    nc.scalar.activation(a_hi[:, i, :], ps[:, i % 4, :], ACT.Copy).then_inc(ch_hi, 1)
                r_squares(0)
                evacuate(E_DFT, ev_q, 6, P, 256)
                store_ev(E_DFT, ev_q)
                for r in range(R_DFT):
                    r_root(r)
                    if r + 1 < R_DFT:
                        r_squares(r + 1)
                    r_store(r)
                for j in range(8):
                    evacuate(E_DFT + 1 + j, ev_q, j // 2, P, 256, col=256 * (j % 2))
                    store_ev(E_DFT + 1 + j, ev_q)
                for e in range(E_QUP, E_V):
                    g, mt = divmod(e - E_QUP, 5)
                    evacuate(e, ev_q, e % 4, 64 if mt == 4 else P, GW, scale=MLA_SCALE)
                    store_ev(e, ev_q)
                    if mt == 2:
                        r_squares(R_DFT + g)
                    if mt == 4:
                        r_root(R_DFT + g)
                        r_store(R_DFT + g)
                for e in range(E_V, EVJ):
                    evacuate(e, ev_q, e % 4, P, GW if e < E_K else KGW)
                    store_ev(e, ev_q)
                    if e == E_V + 6:
                        for r in range(R_NORMED, R_NORMED + 3):
                            r_store(r)
                for r in range(R_NORMED + 3, len(R_JOBS)):
                    r_store(r)

                def exp_tile(pi, s):
                    act.wait_ge(max_done, pi * TILES + s + 1)
                    if s >= 2:
                        act.wait_ge(t_mm, pi * PAIR_CHUNKS + chunks_through(s - 2))
                    n = P if is_ctx(s) else T
                    nc.scalar.activation(probs[:, s % 2, 0:n], s_place(s)[:, 0:n], ACT.Exp,
                                         bias=neg_max[:, s % TILES:s % TILES + 1],
                                         accum_out=exp_sum[:, s % TILES:s % TILES + 1]).then_inc(exp_done, 1)

                def pair(p, first=False, last=False):
                    pi = l * PAIRS + p
                    if first:
                        for s in range(2):
                            exp_tile(pi, s)
                    for s in steps_of(last):
                        r = s - 2
                        out_both(pi, s, first, last)
                        if r < TILES:
                            b, q0 = group_of(r) % 2, P * ((r % 9) % 2)
                            for c, k0, n in chunks_of(r):
                                bank, col = t_place(r, c)
                                act.wait_ge(t_mm, pi * PAIR_CHUNKS + chunk_no(r, c) + 1)
                                if c == 0 and q0 == 0 and (group_of(r) >= 2 or not first):
                                    act.wait_ge(pv_mm, pi * GROUPS + group_of(r) - 1)
                                nc.scalar.activation(pt_hi[:, b, k0:k0 + n, q0:q0 + P],
                                                     ps[:, bank, col:col + n * P].rearrange("p (k t) -> p k t", t=P),
                                                     ACT.Copy).then_inc(pt_hi_done, 1)
                        if s < TILES or not last:
                            exp_tile(pi, s)

                def out_both(pi, s, first, last):
                    g = products_at(s, first, last)
                    if g is not None:
                        n = CTX if g % 5 == 4 else 256
                        act.wait_ge(pv_mm, pi * GROUPS + g + 1)
                        act.wait_ge(o_done, pi * GROUPS + g)
                        nc.scalar.activation(o_both[0:64, 0, 0:n], ps[0:64, 7, 0:n], ACT.Copy)
                        nc.scalar.activation(o_both[0:64, 1, 0:n], ps[64:P, 7, 0:n], ACT.Copy).then_inc(both_done, 1)

                pair(0, first=True)
                with act.Fori(1, 5) as p:
                    pair(p)
                pair(5, last=True)

                norm_x(l * STATS + STATS - G, l * (2 * G * DK) + G * DK, 1, l * (G * DK))
                act.wait_ge(nx_done, (l + 1) * (2 * G * DK))
                settle(act)
                with act.Fori(0, CHUNKS) as c:
                    for j in range(6):
                        n = l * CHUNKS * 6 + c * 6 + j
                        g = j % 3
                        act.wait_ge(gate_mm, n + 1)
                        act.wait_ge(act_f, n + 1)
                        nc.scalar.activation(wk[:, j % 2, :], ps[:, 2 * g, 0:GW], ACT.Silu).then_inc(silu_done, 1)

            act.wait_ge(down_add, DEPTH * CHUNKS * G * DK + 6)
            norm_x(DEPTH * STATS, DEPTH * 2 * G * DK, None)
            for i in range(G * DK):
                g, k = divmod(i, DK)
                act.wait_ge(nx_mul, DEPTH * 2 * G * DK + i + 1)
                nc.scalar.activation(x[:, k, cols(g)], wk[:, i % 4, :], ACT.Copy, scale=vecs[:, 48 + k:49 + k])\
                    .then_inc(y_mod, 1)
            for i in range(9):
                act.wait_ge(y_tr, 2 * i + 1)
                if i >= 2:
                    act.wait_ge(y_stored[i % 2], i // 2 * 16)
                nc.scalar.activation(y_out[:, i % 2, 0:512], ps[:, 0, :], ACT.Copy).then_inc(y_ev_act, 1)

        @block.vector
        def _(dve):
            nc.vector.memset(ones[:, :], 1.0).then_inc(unit_split, STAGES)
            nc.vector.memset(head_ones[:, :], 0.0)
            nc.vector.memset(eps_t[:, 0:1], EPS).then_inc(sq_used, 4)
            nc.vector.memset(eps_t[:, 1:2], 0.0).then_inc(down_add, 6)
            nc.vector.memset(eps_t[:, 2:3], 0.0).then_inc(act_f, 2)
            dve.wait_ge(act_f, 2)
            for q in range(2):
                nc.vector.memset(head_ones[64 * q:64 * q + 64, 64 * q:64 * q + 64], 1.0).then_inc(pre_const, 1)
            dve.wait_ge(pre_tr, 1)
            nc.vector.tensor_copy(vecs[:, 0:74], ps[:, 4, 0:74]).then_inc(pre_vec, 1)
            nc.vector.tensor_copy(b_ada_t[:, :], ps[:, 4, 128:224]).then_inc(pre_vec, 1)
            nc.vector.tensor_copy(chan_hi[:, :], tab_in[:, 0:256]).then_inc(pre_tab, 1)
            nc.vector.tensor_copy(cseq_hi[:, :, :], tab_in[:, 256:512].rearrange("p (c t) -> p c t", c=2))\
                .then_inc(pre_tab, 1)
            dve.wait_ge(pre_tab, 2)
            nc.vector.tensor_tensor(chan_lo[:, :], tab_in[:, 0:256], chan_hi[:, :].bitcast(F32), ALU.subtract)\
                .then_inc(pre_tab, 1)
            nc.vector.tensor_tensor(cseq_lo[:, :, :], tab_in[:, 256:512].rearrange("p (c t) -> p c t", c=2),
                                    cseq_hi[:, :, :].bitcast(F32), ALU.subtract).then_inc(pre_tab, 1)
            for i in range(9):
                dve.wait_ge(x_tr, 2 * i + 2)
                nc.vector.tensor_copy(x[:, 4:8, i * P:(i + 1) * P], ps[:, 1, :].rearrange("p (k t) -> p k t", k=4))\
                    .then_inc(x_ev_dve, 1)
            dve.wait_ge(pre_vec, 2)
            for i in range(DEPTH * ADA_PRE + 1):
                if i < DEPTH * ADA_PRE:
                    dve.wait_ge(ada_mm, i + 1)
                    if i >= 2:
                        dve.wait_ge(ada_tr, i - 1)
                    nc.vector.tensor_copy(pre_row[0:2, i % 2, :], ps[0:2, 2 + i % 2, :]).then_inc(ada_row_done, 1)
                if i:
                    l0, q = divmod(i - 1, ADA_PRE)
                    dve.wait_ge(ada_tr, i)
                    got = ps[:, 4 + (i - 1) % 2, 0:8].rearrange("p (n c) -> p n c", c=2)
                    u0 = 48 * l0 + 4 * q
                    for c in range(2):
                        ins = nc.vector.tensor_tensor(mod[:, u0:u0 + 4, c], got[:, :, c], b_ada_t[:, u0:u0 + 4],
                                                      ALU.add)
                    ins.then_inc(ada_ev, 1)
            dve.wait_ge(ada_ev, DEPTH * ADA_PRE)
            dve.wait_ge(x_ev_act, 9)
            dve.wait_ge(x_ev_dve, 9)

            def newton(stat, slot):
                dve.wait_ge(stat_y0, stat + 1)
                nc.vector.scalar_tensor_tensor(out=nt[:, 2, :], in0=nt[:, 1, :], scalar=-0.5, in1=nt[:, 1, :],
                                               op0=ALU.mult, op1=ALU.mult).then_inc(newt_a, 1)
                dve.wait_ge(newt_a, stat + 1)
                nc.vector.tensor_tensor(nt[:, 2, :], nt[:, 2, :], nt[:, 0, :], ALU.mult).then_inc(newt_b, 1)
                dve.wait_ge(newt_b, stat + 1)
                nc.vector.scalar_tensor_tensor(out=rs[:, slot, :], in0=nt[:, 2, :], scalar=1.5, in1=nt[:, 1, :],
                                               op0=ALU.add, op1=ALU.mult).then_inc(stat_rs, 1)

            def split_norm(n0):
                for i in range(G * DK):
                    g, k = divmod(i, DK)
                    dve.wait_ge(nx_mod, n0 + i + 1)
                    nc.vector.tensor_copy(h_hi[:, k, cols(g)], wk[:, i % 4, :]).then_inc(nx_hi, 1)
                    dve.wait_ge(nx_hi, n0 + i + 1)
                    nc.vector.tensor_tensor(h_lo[:, k, cols(g)], wk[:, i % 4, :], h_hi[:, k, cols(g)].bitcast(F32),
                                            ALU.subtract).then_inc(nx_done, 1)

            with dve.Fori(0, DEPTH) as l:
                steps = [0]

                def link(ins):
                    steps[0] += 1
                    ins.then_inc(dve_step, 1)
                    dve.wait_ge(dve_step, l * DVE_STEPS + steps[0])

                mod_l = mod[:, :, :].rearrange("p (l n) c -> p l n c", l=DEPTH)
                nc.vector.tensor_copy(lmod[:, 0:ADA_FIRST, :], mod_l[:, l, 0:ADA_FIRST])
                nc.vector.tensor_copy(lvec[:, 0:3], vecs[:, 56:62].rearrange("p (l k) -> p l k", l=DEPTH)[:, l])
                nc.vector.tensor_copy(lvec[:, 3:5], vecs[:, 62:66].rearrange("p (l k) -> p l k", l=DEPTH)[:, l])
                nc.vector.tensor_copy(lvec[:, 5:9], vecs[:, 66:74].rearrange("p (v l) -> p l v", l=DEPTH)[:, l])
                nc.vector.tensor_copy(lvec[:, 9:17], vecs[:, 16:32].rearrange("p (l k) -> p l k", l=DEPTH)[:, l])
                link(nc.vector.tensor_copy(lvec[:, 17:25],
                                           vecs[:, 32:48].rearrange("p (l k) -> p l k", l=DEPTH)[:, l]))
                q_gains = lvec[:, 5:9].rearrange("p (a b) -> p a b", b=2)[:, :, 0]
                nc.vector.tensor_scalar(q_gains, q_gains, GQA_SCALE, None, ALU.mult)

                def gain_and_scale(which):
                    for c in range(2):
                        ins = nc.vector.scalar_tensor_tensor(
                            out=gs[:, which, :, c], in0=lmod[:, 24 * which + 8:24 * which + 16, c], scalar=1.0,
                            in1=lvec[:, 9 + 8 * which:17 + 8 * which], op0=ALU.add, op1=ALU.mult)
                    return ins

                gain_and_scale(0).then_inc(lay_ready, 1)
                for g in range(G):
                    newton(l * STATS + g, g)
                split_norm(l * (2 * G * DK))

                def dft_high(i):
                    u = U_DFT + i
                    st, before = u % STAGES, u - RING
                    dve.wait_ge(unit_loaded[st], l * (STAGE_LOADS[st] * 16) + loads_through(u) * 16)
                    if before < U_DFT:
                        dve.wait_ge(ev_mm, l * EVJ + G * (before + 1))
                    else:
                        dve.wait_ge(dft_used, l * (N_DFT - 1) + before - U_DFT + 1)
                    nc.vector.tensor_copy(w_hi[:, u % RING, :], w_in_st[:, st, :]).then_inc(dft_hi, 1)

                for i in range(RING):
                    dft_high(i)
                dve.wait_ge(u_loaded, (l + 1) * 16)
                link(nc.vector.tensor_copy(u_hi[:, :, :], u_raw[:, :, :]))
                nc.vector.tensor_tensor(u_lo[:, :, :], u_raw[:, :, :], u_hi[:, :, :].bitcast(F32), ALU.subtract)\
                    .then_inc(u_split, 1)
                for i in range(9):
                    dve.wait_ge(ch_hi, l * 9 + i + 1)
                    nc.vector.tensor_tensor(a_lo[:, i, :], ps[:, i % 4, :], a_hi[:, i, :].bitcast(F32), ALU.subtract)\
                        .then_inc(ch_lo, 1)

                def r_job(r):
                    kind, t, g = R_JOBS[r]
                    s, raw = raw_slot(r), raw_of(r)
                    if kind in ("gk", "gq"):
                        v = 5 if kind == "gq" else 6
                        dve.wait_ge(r_loaded[s], l * RL_TOTAL[s] + RL_AFTER[r])
                        dve.wait_ge(r_sq, l * R_NORMED + r + 1)
                        nc.vector.scalar_tensor_tensor(out=raw[:, 0, :], in0=raw[:, 0, :], scalar=lvec[:, v:v + 1],
                                                       in1=raw[:, 2, :], op0=ALU.mult, op1=ALU.mult)
                        link(nc.vector.scalar_tensor_tensor(out=raw[:, 1, :], in0=raw[:, 1, :],
                                                            scalar=lvec[:, v + 2:v + 3], in1=raw[:, 3, :],
                                                            op0=ALU.mult, op1=ALU.mult))
                        link(nc.vector.tensor_tensor(raw[:, 0, :], raw[:, 0, :], raw[:, 1, :], ALU.add))
                    if r < R_NORMED:
                        newton(l * STATS + G + r, r % 3)
                        dve.wait_ge(stat_rs, l * STATS + G + r + 1)
                    else:
                        dve.wait_ge(r_loaded[s], l * RL_TOTAL[s] + RL_AFTER[r])
                    for n, (r_, i, k) in enumerate(R_USES):
                        if r_ != r:
                            continue
                        slot = n % RO_SLOTS
                        out = r_out[:, slot, :]
                        before = RO_AFTER[n - RO_SLOTS] if n >= RO_SLOTS else 0
                        dve.wait_ge(r_stored[slot], l * RO_TOTAL[slot] + before)
                        root_, last = rs[:, r % 3, :], None
                        if kind in ("cq", "ckv"):
                            gain = lvec[:, i:i + 1] if kind == "cq" else lvec[:, 3 + i:4 + i]
                            last = nc.vector.scalar_tensor_tensor(out=out, in0=raw[:, i, :], scalar=gain, in1=root_,
                                                                  op0=ALU.mult, op1=ALU.mult)
                            if kind == "ckv":
                                link(last)
                                last = None
                                for c0, c1, k0 in key_pieces(g):
                                    link(nc.vector.tensor_copy(ckv_hi[:, i, k0:k0 + c1 - c0], out[:, c0:c1]))
                                for c0, c1, k0 in key_pieces(g):
                                    k1 = k0 + c1 - c0
                                    ins = nc.vector.tensor_tensor(ckv_lo[:, i, k0:k1], out[:, c0:c1],
                                                                  ckv_hi[:, i, k0:k1].bitcast(F32), ALU.subtract)
                                ins.then_inc(r_use, 1)
                        elif kind in ("gk", "gq"):
                            last = nc.vector.tensor_tensor(out, raw[:, 0, :], root_, ALU.mult)
                        else:
                            m = 96 if t == 1 else P
                            nc.vector.tensor_tensor(raw[0:m, 0, :], raw[0:m, 0, :], raw[0:m, 2, :], ALU.mult)
                            link(nc.vector.tensor_tensor(raw[0:m, 1, :], raw[0:m, 1, :], raw[0:m, 3, :], ALU.mult))
                            last = nc.vector.tensor_tensor(out[0:m, :], raw[0:m, 0, :], raw[0:m, 1, :], ALU.add)
                        if last is not None:
                            last.then_inc(r_use, 1)
                    return last

                def r_end(r):
                    steps_of = [n for n, (r_, _, _) in enumerate(R_USES) if r_ == r]
                    dve.wait_ge(r_use, l * len(R_USES) + steps_of[-1] + 1)
                    nc.vector.memset(eps_t[:, 3:4], 0.0).then_inc(r_dve, 1)

                for r in range(R_DFT):
                    if 1 <= r <= N_DFT - RING:
                        dft_high(RING + r - 1)
                    r_job(r)
                    r_end(r)
                dve.wait_ge(cq_loaded, (l + 1) * 16)
                link(nc.vector.tensor_copy(cq_hi[:, :, :], cq_raw[:, :, :]))
                dve.wait_ge(ev_mm, l * EVJ + E_QUP)
                for g in range(G):
                    nc.vector.tensor_tensor(cq_lo[:, :, cols(g)], cq_raw[:, :, cols(g)],
                                            cq_hi[:, :, cols(g)].bitcast(F32), ALU.subtract).then_inc(cq_split, 1)
                for r in range(R_DFT, R_NORMED):
                    r_job(r)
                    n = [n for n, (r_, _, _) in enumerate(R_USES) if r_ == r][-1]
                    dve.wait_ge(r_use, l * len(R_USES) + n + 1)
                    nc.vector.memset(eps_t[:, 3:4], 0.0).then_inc(r_dve, 1)
                    nc.vector.memset(eps_t[:, 4:5], 0.0).then_inc(ckv_split, 1)
                for i in range(2):
                    dve.wait_ge(tr_mm, l * 5 + i + 1)
                    link(nc.vector.tensor_copy(ckv_hi[:, i, CTX:CTX + PAST], ps[:, 6 + i, 0:P]))
                    nc.vector.tensor_tensor(ckv_lo[:, i, CTX:CTX + PAST], ps[:, 6 + i, 0:P],
                                            ckv_hi[:, i, CTX:CTX + PAST].bitcast(F32), ALU.subtract)\
                        .then_inc(tr_ev, 1)
                dve.wait_ge(tr_ev, l * 5 + 2)
                nc.vector.memset(eps_t[:, 4:5], 0.0).then_inc(ckv_split, 1)
                dve.wait_ge(tr_mm, l * 5 + 3)
                nc.vector.tensor_copy(cache_t[0:ROPE, 0, :], ps[0:ROPE, 6, 0:P]).then_inc(tr_ev, 1)
                dve.wait_ge(tr_mm, l * 5 + 4)
                nc.vector.tensor_copy(cache_t[:, 1, :], ps[:, 7, 0:P]).then_inc(tr_ev, 1)
                for r in range(R_NORMED, len(R_JOBS)):
                    r_job(r)
                    r_end(r)
                def inverse(pi, s):
                    dve.wait_ge(exp_done, pi * TILES + s + 1)
                    i = s % TILES
                    nc.vector.reciprocal(exp_inv[:, i:i + 1], exp_sum[:, i:i + 1]).then_inc(inv_done, 1)

                def high_steps(mla, tiles_done, groups_done, y):
                    rows = 96 if mla else P
                    qh, kh, v2 = (mq_hi, mk_hi, mv) if mla else (gq2, gk2, gv2)

                    def q_high():
                        dve.wait_ge(q_loaded, (y + 1) * 32)
                        dve.wait_ge(s_mm, tiles_done)
                        nc.vector.tensor_copy(qh[0:rows, :], qst[0:rows, :]).then_inc(prep_hi, 1)

                    def k_high():
                        dve.wait_ge(k_loaded, (y + 1) * 32)
                        nc.vector.tensor_copy(kh[0:rows, :], kst[0:rows, :]).then_inc(prep_hi, 1)

                    def v_high():
                        dve.wait_ge(v_loaded, (y + 1) * 16)
                        dve.wait_ge(pv_mm, groups_done)
                        nc.vector.tensor_copy(v2[:, :, 0:VD], vst[:, :, :]).then_inc(prep_hi, 1)

                    return q_high, k_high, v_high

                for step in high_steps(True, l * PAIRS * TILES, l * PAIRS * GROUPS, l * 12):
                    step()

                def max_tile(pi, s):
                    dve.wait_ge(s_mm, pi * TILES + s + 1)
                    n = P if is_ctx(s) else T
                    nc.vector.tensor_reduce(neg_max[:, s % TILES:s % TILES + 1], s_place(s)[:, 0:n], AX_X, ALU.max,
                                            negate=True).then_inc(max_done, 1)

                def out_sum(pi, s, first, last):
                    g = products_at(s, first, last)
                    if g is not None:
                        n = CTX if g % 5 == 4 else 256
                        dve.wait_ge(both_done, pi * GROUPS + g + 1)
                        if g >= 2 or not first:
                            dve.wait_ge(o_stored[g % 2], (pi * (GROUPS // 2) + g // 2) * 16)
                        nc.vector.tensor_tensor(o_sum[0:64, g % 2, 0:n], o_both[0:64, 0, 0:n],
                                                o_both[0:64, 1, 0:n], ALU.add)\
                            .then_inc(o_done, 1)

                def ada_chunk(p, w):
                    n = l * ADA_LATE + (p - 1) * 2 + w
                    dve.wait_ge(late_mm, n + 1)
                    nc.vector.tensor_copy(ada_row[0:2, :], ps[0:2, 6, :]).then_inc(late_row, 1)
                    dve.wait_ge(late_tr, n + 1)
                    got = ps[:, 6, 0:8].rearrange("p (n c) -> p n c", c=2)
                    dst = mod[:, :, :].rearrange("p (l q n) c -> p l q n c", l=DEPTH, n=4)
                    bias = b_ada_t[:, :].rearrange("p (l q n) -> p l q n", l=DEPTH, n=4)
                    q = (p - 1) * 2 + ADA_PRE + w
                    for c in range(2):
                        ins = nc.vector.tensor_tensor(dst[:, l, q, :, c], got[:, :, c], bias[:, l, q, :], ALU.add)
                    ins.then_inc(late_ev, 1)

                def pair(p, first=False, last=False):
                    pi = l * PAIRS + p
                    steps = [high_steps(False, pi * TILES, pi * GROUPS, pi * 2 + 1),
                             () if last else high_steps(True, pi * TILES + 9, pi * GROUPS + 5, pi * 2 + 2)]
                    if first:
                        for s in range(2):
                            max_tile(pi, s)
                            if s:
                                inverse(pi, 0)
                    for s in steps_of(last):
                        r = s - 2
                        if s < TILES and s % 9 + 1 in PREP_AT and steps[s // 9]:
                            steps[s // 9][PREP_AT.index(s % 9 + 1)]()
                        if s < TILES or not last:
                            max_tile(pi, s)
                        if s <= TILES or not last:
                            inverse(pi, s - 1)
                        if r < TILES:
                            b, q0 = group_of(r) % 2, P * ((r % 9) % 2)
                            for c, k0, n in chunks_of(r):
                                bank, col = t_place(r, c)
                                dve.wait_ge(pt_hi_done, pi * PAIR_CHUNKS + chunk_no(r, c) + 1)
                                nc.vector.tensor_tensor(
                                    pt_lo[:, b, k0:k0 + n, q0:q0 + P],
                                    ps[:, bank, col:col + n * P].rearrange("p (k t) -> p k t", t=P),
                                    pt_hi[:, b, k0:k0 + n, q0:q0 + P].bitcast(F32), ALU.subtract)\
                                    .then_inc(pt_lo_done, 1)
                        out_sum(pi, s, first, last)
                        if not first and not last and s in ADA_AT:
                            ada_chunk(p, ADA_AT.index(s))

                pair(0, first=True)
                with dve.Fori(1, 5) as p:
                    pair(p)
                pair(5, last=True)
                dve.wait_ge(late_ev, (l + 1) * ADA_LATE)
                nc.vector.memset(eps_t[:, 5:6], 0.0)
                link(nc.vector.tensor_copy(lmod[:, ADA_FIRST:48, :], mod_l[:, l, ADA_FIRST:48]))
                link(gain_and_scale(1))

                for i in range(G * DK):
                    g, k = divmod(i, DK)
                    dve.wait_ge(mix_loaded[i % 4], l * (G * DK // 4 * 16) + (i // 4 + 1) * 16)
                    nc.vector.tensor_copy(h_hi[:, k, cols(g)], wk[:, i % 4, :]).then_inc(mix_hi, 1)
                    dve.wait_ge(mix_hi, l * G * DK + i + 1)
                    nc.vector.tensor_tensor(h_lo[:, k, cols(g)], wk[:, i % 4, :], h_hi[:, k, cols(g)].bitcast(F32),
                                            ALU.subtract).then_inc(mix_split, 1)

                def add_gated(m, g, gate, bank, done):
                    for c, c0, c1 in halves(g):
                        ins = nc.vector.scalar_tensor_tensor(
                            out=x[:, m, c0:c1], in0=ps[:, bank, c0 - g * GW:c1 - g * GW],
                            scalar=lmod[:, gate + m, c:c + 1], in1=x[:, m, c0:c1], op0=ALU.mult, op1=ALU.add)
                    ins.then_inc(done, 1)

                for n in range(G * DK):
                    m, g = divmod(n, G)
                    dve.wait_ge(out_mm, l * G * DK + n + 1)
                    add_gated(m, g, 16, n % 4, out_add)
                    if n == 7:
                        dve.wait_ge(tr_mm, (l + 1) * 5)
                        nc.vector.tensor_copy(nat_out[:, :], ps[:, 4, 0:416]).then_inc(tr_ev, 1)
                for g in range(G):
                    newton(l * STATS + STATS - G + g, g)
                split_norm(l * (2 * G * DK) + G * DK)
                dve.wait_ge(nat_stored, (l + 1) * 48)
                nc.vector.memset(eps_t[:, 5:6], 0.0)
                with dve.Fori(0, CHUNKS) as c:
                    for j in range(6):
                        t, g = divmod(j, G)
                        n = l * (CHUNKS * 6) + c * 6 + j
                        dve.wait_ge(silu_done, n + 1)
                        dve.wait_ge(up_mm, n + 1)
                        nc.vector.tensor_tensor(wk[:, 2 + j % 2, :], ps[:, 2 * g + 1, 0:GW], wk[:, j % 2, :], ALU.mult)\
                            .then_inc(act_f, 1)
                        dve.wait_ge(act_f, n + 3)
                        nc.vector.tensor_copy(act_hi[:, t, cols(g)], wk[:, 2 + j % 2, :]).then_inc(act_h, 1)
                        dve.wait_ge(act_h, n + 1)
                        nc.vector.tensor_tensor(act_lo[:, t, cols(g)], wk[:, 2 + j % 2, :],
                                                act_hi[:, t, cols(g)].bitcast(F32), ALU.subtract).then_inc(act_done, 1)
                    for d in range(G * DK):
                        g, m = divmod(d, DK)
                        dve.wait_ge(down_mm, l * (CHUNKS * G * DK) + c * (G * DK) + d + 1)
                        add_gated(m, g, 40, d % 6, down_add)
                dve.wait_ge(down_add, (l + 1) * (CHUNKS * G * DK) + 6)
                assert steps[0] == DVE_STEPS, steps[0]

            for g in range(G):
                newton(DEPTH * STATS + g, g)
            for i in range(9):
                dve.wait_ge(y_tr, 2 * i + 2)
                if i >= 2:
                    dve.wait_ge(y_stored[i % 2], i // 2 * 16)
                nc.vector.tensor_copy(y_out[:, i % 2, 512:1024], ps[:, 1, :]).then_inc(y_ev_dve, 1)

        @block.tensor
        def _(pe):
            def mm3(out, wh, wl, xh, xl, first, last):
                nc.tensor.matmul(out, wh, xh, start=first, stop=False)
                nc.tensor.matmul(out, wh, xl, start=False, stop=False)
                return nc.tensor.matmul(out, wl, xh, start=False, stop=last)

            pe.wait_ge(pre_ident, 2)
            pe.wait_ge(pre_const, 2)
            pe.wait_ge(pre_loaded, PRE_LOADS * 16)
            nc.tensor.transpose(ps[:, 4, 0:74], vec_rows[0:74, :], ident[0:74, 0:74])
            nc.tensor.transpose(ps[:, 4, 128:224], ada_rows[:, :], ident[0:96, 0:96]).then_inc(pre_tr, 1)
            for i in range(9):
                pe.wait_ge(x_loaded[i % 2], (i // 2 + 1) * 16)
                for half in range(2):
                    pe.wait_ge((x_ev_act, x_ev_dve)[half], i)
                    for j in range(4):
                        k = 4 * half + j
                        ins = nc.tensor.transpose(ps[:, half, j * P:(j + 1) * P], x_in[:, i % 2, k * P:(k + 1) * P],
                                                  ident[:, :])
                    ins.then_inc(x_tr, 1)
            pe.wait_ge(pre_silu, 1)
            for i in range(DEPTH * ADA_PRE + 1):
                if i < DEPTH * ADA_PRE:
                    pe.wait_ge(ada_loaded[i % ADA_SLOTS], (i // ADA_SLOTS + 1) * 16)
                    if i >= 2:
                        pe.wait_ge(ada_row_done, i - 1)
                    for k in range(DK):
                        ins = nc.tensor.matmul(ps[0:2, 2 + i % 2, :], silu_c[:, :, k], ada_w[:, i % ADA_SLOTS, k, :],
                                               start=(k == 0), stop=(k == DK - 1))
                    ins.then_inc(ada_mm, 1)
                if i:
                    pe.wait_ge(ada_row_done, i)
                    if i >= 3:
                        pe.wait_ge(ada_ev, i - 2)
                    for j in range(4):
                        ins = nc.tensor.transpose(ps[:, 4 + (i - 1) % 2, 2 * j:2 * j + 2],
                                                  pre_row[0:2, (i - 1) % 2, j * P:(j + 1) * P], ident[0:2, 0:2])
                    ins.then_inc(ada_tr, 1)

            def sum_square(n0, i, g, k):
                pe.wait_ge(sq_done, n0 + i + 1)
                nc.tensor.matmul(ps[:, 5 + g, 0:GW], ones[:, :], wk[:, i % 4, :], start=(k == 0),
                                 stop=(k == DK - 1)).then_inc(sq_used, 1)

            def sum_squares(n0):
                for i in range(G * DK):
                    sum_square(n0, i, *divmod(i, DK))

            with pe.Fori(0, DEPTH) as l:
                def unit(u, n):
                    pe.wait_ge(unit_split, l * UNITS + u + 1 + STAGES)
                    return wtiles(u, n)

                sum_squares(l * (2 * G * DK))
                for u, (name, _, w) in enumerate(IN_TILES):
                    wh, wl = unit(u, w)
                    for g in range(G):
                        e = G * u + g
                        if u == 0:
                            pe.wait_ge(nx_done, l * (2 * G * DK) + (g + 1) * DK)
                        if e >= 6:
                            pe.wait_ge(ev_done, l * EVJ + e - 5)
                        if name == "gv":
                            for i in range(3):
                                t0 = g * GW + i * P
                                out = ps[:, e % 6, i * P:(i + 1) * P]
                                for k in range(DK):
                                    ins = mm3(out, h_hi[:, k, t0:t0 + P], h_lo[:, k, t0:t0 + P], wh[:, k, :],
                                              wl[:, k, :], k == 0, k == DK - 1)
                        else:
                            for k in range(DK):
                                ins = mm3(ps[0:w, e % 6, 0:GW], wh[:, k, :], wl[:, k, :], h_hi[:, k, cols(g)],
                                          h_lo[:, k, cols(g)], k == 0, k == DK - 1)
                        ins.then_inc(ev_mm, 1)

                pe.wait_ge(u_split, l + 1)
                pe.wait_ge(ev_done, l * EVJ + E_DFT)
                pe.wait_ge(pre_tab, 4)
                for i in range(9):
                    if i >= 4:
                        pe.wait_ge(ch_lo, l * 9 + i - 3)
                    for f in range(2):
                        ts = slice(i * P, (i + 1) * P)
                        ins = mm3(ps[:, i % 4, 256 * f:256 * f + 256], u_hi[:, f, ts], u_lo[:, f, ts], chan_hi[:, :],
                                  chan_lo[:, :], True, True)
                    ins.then_inc(ch_mm, 1)
                pe.wait_ge(ch_lo, l * 9 + 9)

                def a_part(i, f, cs):
                    c0 = 256 * f + 128 * cs
                    return a_hi[:, i, c0:c0 + P], a_lo[:, i, c0:c0 + P]

                for f in range(2):
                    for cs in range(2):
                        ah, al = a_part(0, f, cs)
                        ins = mm3(ps[:, 6, P * f:P * f + P], ah, al, cseq_hi[:, cs, :], cseq_lo[:, cs, :],
                                  cs == 0, cs == 1)
                ins.then_inc(ev_mm, 1)

                def r_stat(r):
                    kind, t, g = R_JOBS[r]
                    k = {"cq": 3, "ckv": 2}.get(kind, 1)
                    pe.wait_ge(r_sq, l * R_NORMED + r + 1)
                    if r >= 2:
                        pe.wait_ge(stat_y0, l * STATS + G + r - 1)
                    for i in range(k):
                        ins = nc.tensor.matmul(ps[:, 4 + r % 2, 0:GW], (ones if k > 1 else head_ones)[:, :],
                                               wk[:, sq_slot(r) + i, :], start=(i == 0), stop=(i == k - 1))
                    ins.then_inc(stat_mm, 1)

                for i in range(N_DFT):
                    wh, wl = unit(U_DFT + i, 512)
                    for f in range(2):
                        ah, al = a_part(1 + i // 2, f, i % 2)
                        for half in range(2):
                            ins = mm3(ps[:, 2 * f + half, :], ah, al, wh[:, half, :], wl[:, half, :],
                                      i == 0, i == N_DFT - 1)
                            if i == N_DFT - 1:
                                ins.then_inc(ev_mm, 2)
                    if i < N_DFT - 1:
                        ins.then_inc(dft_used, 1)
                    if i < R_DFT:
                        r_stat(i)

                uq = [unit(U_QUP + k, HEADS * (NOPE + ROPE)) for k in range(N_QUP)]
                for e in range(E_QUP, E_V):
                    g, mt = divmod(e - E_QUP, 5)
                    if mt == 0:
                        pe.wait_ge(cq_split, l * G + g + 1)
                    if e < E_QUP + 4:
                        pe.wait_ge(ev_done, l * EVJ + E_DFT + 1 + 2 * (e % 4 + 1))
                    else:
                        pe.wait_ge(ev_done, l * EVJ + e - 3)
                    m = 64 if mt == 4 else P
                    for k in range(N_QUP):
                        wh, wl = (t[:, 0, mt * P:mt * P + m] for t in uq[k])
                        ins = mm3(ps[0:m, e % 4, 0:GW], wh, wl, cq_hi[:, k, cols(g)], cq_lo[:, k, cols(g)],
                                  k == 0, k == N_QUP - 1)
                    ins.then_inc(ev_mm, 1)
                    if mt == 4:
                        r_stat(R_DFT + g)
                pe.wait_ge(cache_loaded, (l + 1) * 48)
                for i, (c0, w) in enumerate(((0, P), (P, P), (256, ROPE), (288, P))):
                    if i >= 2:
                        pe.wait_ge(tr_ev, l * 5 + i - 1)
                        settle(pe)
                    nc.tensor.transpose(ps[0:w, 6 + i % 2, 0:P], cache_in[:, c0:c0 + w], ident[:, :]).then_inc(tr_mm, 1)
                uk = [unit(U_KVUP + k, HEADS * (NOPE + VD)) for k in range(N_KVUP)]
                for e in range(E_V, EVJ):
                    pe.wait_ge(ev_done, l * EVJ + e - 3)
                    if e < E_K:
                        kt = V_ORDER[e - E_V]
                        pe.wait_ge(ckv_split, l * 4 + (4 if kt == 1 else 1 + max(kt - 1, 0) // 3))
                        ks = slice(kt * P, (kt + 1) * P)
                        for k in range(N_KVUP):
                            wh, wl = (t[:, 0, HEADS * NOPE:] for t in uk[k])
                            ins = mm3(ps[:, e % 4, 0:HEADS * VD], ckv_hi[:, k, ks], ckv_lo[:, k, ks], wh, wl,
                                      k == 0, k == N_KVUP - 1)
                    else:
                        mt, kg = divmod(e - E_K, KG)
                        ks = slice(kg * KGW, (kg + 1) * KGW)
                        for k in range(N_KVUP):
                            wh, wl = (t[:, 0, mt * P:(mt + 1) * P] for t in uk[k])
                            ins = mm3(ps[:, e % 4, 0:KGW], wh, wl, ckv_hi[:, k, ks], ckv_lo[:, k, ks],
                                      k == 0, k == N_KVUP - 1)
                    ins.then_inc(ev_mm, 1)
                pe.wait_ge(ev_done, (l + 1) * EVJ)
                pe.wait_ge(tr_ev, l * 5 + 4)
                settle(pe)

                def scores(pi, s, first):
                    mla, t = s % TILES < 9, s % 9
                    if t == 0:
                        pe.wait_ge(prep_q, pi * 2 + s // 9 + 1)
                        pe.wait_ge(prep_k, pi * 2 + s // 9 + 1)
                    if s >= 2:
                        pe.wait_ge(exp_done, pi * TILES + s - 1)
                    q0 = 0 if is_ctx(s) else CTX + t * P
                    qs = slice(q0, q0 + P)
                    parts = [(0, P, 0)] if is_ctx(s) else [(0, 512, CTX), (512, 512, CTX + 512),
                                                           (1024, P, CTX + 1024)]
                    for c0, n, k0 in parts:
                        if c0 == 1024 and s >= 3 - (not first):
                            pe.wait_ge(pt_lo_done, pi * PAIR_CHUNKS + chunk_no(s - 3) + 1)
                        out, ks = s_place(s)[:, c0:c0 + n], slice(k0, k0 + n)
                        if mla:
                            ins = mm3(out, mq_hi[0:96, qs], mq_lo[0:96, qs], mk_hi[0:96, ks], mk_lo[0:96, ks],
                                      True, True)
                        else:
                            nc.tensor.matmul(out, gq2[:, qs], gk2[:, ks], start=True, stop=False)
                            ins = nc.tensor.matmul(out, gq2[0:64, qs], gk_lo[0:64, ks], start=False, stop=True)
                    ins.then_inc(s_mm, 1)

                def products(pi, g, s):
                    if g % 5 == 0:
                        pe.wait_ge(prep_v, pi * 2 + 1 + g // 5)
                    pe.wait_ge(pt_lo_done, pi * PAIR_CHUNKS + chunks_through(min(s - 3, TILES - 1)))
                    pe.wait_ge(both_done, pi * GROUPS + g)
                    v2 = mv if g % GROUPS < 5 else gv2
                    n, tiles_, kt0 = (CTX, 1, 0) if g % 5 == 4 else (256, 9, 1)
                    for kt in range(tiles_):
                        for part, pt in enumerate((pt_hi, pt_lo)):
                            ins = nc.tensor.matmul(ps[:, 7, 0:n], v2[:, kt0 + kt, :], pt[:, g % 2, kt, 0:n],
                                                   start=(kt == 0 and part == 0),
                                                   stop=(kt == tiles_ - 1 and part == 1))
                    ins.then_inc(pv_mm, 1)

                def pair(p, first=False, last=False):
                    pi = l * PAIRS + p
                    if first:
                        for s in range(2):
                            scores(pi, s, first)
                    for s in steps_of(last):
                        if s < TILES or not last:
                            scores(pi, s, first)
                        g = products_at(s, first, last)
                        r = s - 2
                        if g is not None:
                            products(pi, g, s)
                        if r >= TILES:
                            continue
                        pe.wait_ge(p_done, pi * TILES + r + 1)
                        for c, k0, n in chunks_of(r):
                            bank, col = t_place(r, c)
                            if c == 0 and (s - 1 < TILES or not last):
                                pe.wait_ge(exp_done, pi * TILES + s)
                            if c == 1 and (r >= 1 or not first):
                                pe.wait_ge(pt_lo_done, pi * PAIR_CHUNKS + chunks_through(r - 1))
                            if c == 1 and r == 9 and not first and not last:
                                pe.wait_ge(late_ev, l * ADA_LATE + (p - 1) * 2 + 1)
                            if c == 1 and r == 0 and not first:
                                pe.wait_ge(late_ev, l * ADA_LATE + (ADA_LATE if last else p * 2 - 2))
                            if c == 2 and g is not None:
                                pe.wait_ge(both_done, pi * GROUPS + g + 1)
                            for j in range(n):
                                kt = k0 + j
                                ins = nc.tensor.transpose(ps[:, bank, col + j * P:col + (j + 1) * P],
                                                          probs[:, r % 2, kt * P:(kt + 1) * P], ident[:, :])
                            ins.then_inc(t_mm, 1)
                        if not first and not last and s in ADA_AT:
                            ada_chunk(p, ADA_AT.index(s))

                def ada_chunk(p, w):
                    pi = l * PAIRS + p
                    n = l * ADA_LATE + (p - 1) * 2 + w
                    pe.wait_ge(late_loaded[w], l * (4 * 64) + p * 64)
                    pe.wait_ge(pt_lo_done, pi * PAIR_CHUNKS + chunks_through(ADA_AT[w] - 3))
                    for k in range(DK):
                        ins = nc.tensor.matmul(ps[0:2, 6, :], silu_c[:, :, k], ada_buf[:, w, k, :],
                                               start=(k == 0), stop=(k == DK - 1))
                    ins.then_inc(late_mm, 1)
                    pe.wait_ge(late_row, n + 1)
                    settle(pe)
                    for j in range(4):
                        ins = nc.tensor.transpose(ps[:, 6, 2 * j:2 * j + 2], ada_row[0:2, j * P:(j + 1) * P],
                                                  ident[0:2, 0:2])
                    ins.then_inc(late_tr, 1)

                pair(0, first=True)
                with pe.Fori(1, 5) as p:
                    pair(p)
                pair(5, last=True)

                norm2 = l * (2 * G * DK) + G * DK
                for n in range(G * DK + 4):
                    if n < G * DK:
                        m, g = divmod(n, G)
                        if g == 0:
                            wh, wl = unit(U_OUT + m, P)
                        if m == 0:
                            pe.wait_ge(mix_split, l * G * DK + (g + 1) * DK)
                        if n >= 4:
                            pe.wait_ge(out_add, l * G * DK + n - 3)
                        for k in range(DK):
                            ins = mm3(ps[:, n % 4, 0:GW], wh[:, k, :], wl[:, k, :], h_hi[:, k, cols(g)],
                                      h_lo[:, k, cols(g)], k == 0, k == DK - 1)
                        ins.then_inc(out_mm, 1)
                    if n >= 4:
                        k, g = divmod(n - 4, G)
                        sum_square(norm2, n - 4, g, k)
                    if n == 6:
                        pe.wait_ge(ctx_loaded, (l + 1) * 48)
                        settle(pe)
                        for i, (c0, w) in enumerate(((0, P), (P, P), (256, ROPE), (288, P))):
                            ins = nc.tensor.transpose(ps[:, 4, c0:c0 + w], ctx_in[0:w, i, :], ident[0:w, 0:w])
                        ins.then_inc(tr_mm, 1)
                with pe.Fori(0, CHUNKS) as c:
                    c6 = l * (CHUNKS * 6) + c * 6
                    c24 = l * (CHUNKS * G * DK) + c * (G * DK)

                    def ffn_unit(j, n):
                        pe.wait_ge(unit_split, l * UNITS + c * 6 + U_FFN + j + 1 + STAGES)
                        return wtiles(j, n)

                    for t in range(2):
                        gate, up = ffn_unit(2 * t, P), ffn_unit(2 * t + 1, P)
                        for g in range(G):
                            j = 3 * t + g
                            for b, (w, done) in enumerate(((gate, gate_mm), (up, up_mm))):
                                if t == 0:
                                    pe.wait_ge(down_add, c24 + 2 * g + b + 1)
                                    if b == 0:
                                        pe.wait_ge(nx_done, norm2 + (g + 1) * DK)
                                elif b == 0:
                                    pe.wait_ge(silu_done, c6 + j - 2)
                                else:
                                    pe.wait_ge(act_f, c6 + j)
                                for k in range(DK):
                                    ins = mm3(ps[:, 2 * g + b, 0:GW], w[0][:, k, :], w[1][:, k, :], h_hi[:, k, cols(g)],
                                              h_lo[:, k, cols(g)], k == 0, k == DK - 1)
                                ins.then_inc(done, 1)
                    down = ffn_unit(4, 512), ffn_unit(5, 512)
                    for d in range(G * DK):
                        g, m = divmod(d, DK)
                        if m == 0:
                            pe.wait_ge(act_done, c6 + 3 + g + 1)
                        if d >= 6:
                            pe.wait_ge(down_add, c24 + d + 1)
                        elif d % 2 == 0:
                            pe.wait_ge(silu_done, c6 + 3 + d // 2 + 1)
                        else:
                            pe.wait_ge(act_f, c6 + 3 + d // 2 + 3)
                        wh, wl = down[m // 4]
                        m0 = (m % 4) * P
                        for t in range(2):
                            ins = mm3(ps[:, d % 6, 0:GW], wh[:, t, m0:m0 + P], wl[:, t, m0:m0 + P],
                                      act_hi[:, t, cols(g)], act_lo[:, t, cols(g)], t == 0, t == 1)
                        ins.then_inc(down_mm, 1)

            sum_squares(DEPTH * 2 * G * DK)
            for i in range(9):
                pe.wait_ge(y_mod, (i // 3 + 1) * DK)
                for half in range(2):
                    pe.wait_ge((y_ev_act, y_ev_dve)[half], i)
                    for j in range(4):
                        ins = nc.tensor.transpose(ps[:, half, j * P:(j + 1) * P],
                                                  x[:, 4 * half + j, i * P:(i + 1) * P], ident[:, :])
                    ins.then_inc(y_tr, 1)


def tables():
    def dft(n, sign):
        k = np.arange(n)
        ang = 2 * np.pi * (np.outer(k, k) % n) / n
        return np.cos(ang), sign * np.sin(ang)

    c64, s64 = dft(64, 1.0)
    chan = np.zeros((P, 2, P))
    for i, t in enumerate((c64, s64)):
        for b in range(2):
            chan[64 * b:64 * b + 64, i, 64 * b:64 * b + 64] = t / 8.0
    c, s = dft(CTX, -1.0)
    t_ctx = np.stack([c, s], axis=1) / np.sqrt(CTX)
    c, s = dft(LAT, -1.0)
    t_seq = np.stack([c, s], axis=1).reshape(LAT // P, P, 2, LAT) / 32.0

    def rope(dim, copies):
        f = np.float32
        n_axis = dim // 4
        inv = (f(10000.0) ** (-np.arange(n_axis, dtype=f) / f(n_axis))).astype(f)
        t = np.arange(LAT)
        ang = np.concatenate([(t // GRID_W).astype(f)[:, None] * inv, (t % GRID_W).astype(f)[:, None] * inv], axis=1)
        cos, sin = np.cos(ang.astype(np.float64)).T, np.sin(ang.astype(np.float64)).T
        out = np.zeros((P, 2, T))
        out[:, 0, :CTX] = 1.0
        out[:, 0, CTX:] = np.tile(np.concatenate([cos, cos]), (copies, 1))
        out[:, 1, CTX:] = np.tile(np.concatenate([-sin, sin]), (copies, 1))
        return out

    f = {"t_chan": chan.reshape(P, 256), "t_ctx": t_ctx.reshape(P, 256), "t_seq": t_seq,
         "t_rope_gqa": rope(64, 2), "t_rope_mla": rope(32, 4)}
    return {k: np.ascontiguousarray(v, dtype=np.float32) for k, v in f.items()}


_INS = ["x_prompt", "x_sample", "cache_mla_ckv", "cache_mla_krope", "cache_gqa_k", "cache_gqa_v", "c", "c_ctx",
        "w_ada", "b_ada", "g_norm1", "g_norm2", "w_in", "g_q_a", "w_q_up", "g_kv_a", "w_kv_up", "g_q_head",
        "g_k_head", "w_out", "w_ffn_gate", "w_ffn_up", "w_ffn_down", "g_final"]
_OUTS = [("y_prompt", (1, CTX, D_MODEL)), ("y_sample", (1, LAT, D_MODEL)), ("new_mla_ckv", (1, DEPTH, CTX, KVR)),
         ("new_mla_krope", (1, DEPTH, CTX, ROPE)), ("new_gqa_k", (1, DEPTH, CTX, 2, 64)),
         ("new_gqa_v", (1, DEPTH, CTX, 2, 64))]


def kernel(**inputs):
    import concourse.bacc as bacc
    from concourse.bass_utils import run_bass_kernel_spmd

    nc = bacc.Bacc("TRN2", target_bir_lowering=False, num_devices=1)
    arrays, a, o = {}, {}, {}
    for name, value in [(n, inputs[n]) for n in _INS] + list(tables().items()):
        value = np.ascontiguousarray(value)
        arrays[f"in_{name}"] = value
        a[name] = nc.dram_tensor(f"in_{name}", value.shape, mybir.dt.from_np(value.dtype), kind="ExternalInput").ap()
    for name, shape in _OUTS:
        o[name] = nc.dram_tensor(f"out_{name}", shape, F32, kind="ExternalOutput").ap()
    build(nc, a, o)
    r = run_bass_kernel_spmd(nc, [arrays], core_ids=[0])
    return tuple(r.results[0][f"out_{name}"] for name, _ in _OUTS)
```
